# Optimizing a Trainium2 kernel written in Bass

```python
import math
import jax
import jax.numpy as jnp
from jax import lax
import numpy as np

D_MODEL = 1024
BATCH = 1
SEQ = 1024
DEPTH = 1

CHUNK = 64
N_META = 16
D_MIX = D_MODEL
EPS = 1e-6
CONV_CH = D_MIX // 2
CONV_GROUPS = 8
CONV_K_MIX = 3
GDN_HEADS = 4
GDN_HEAD_DIM = 128
GDN_W = GDN_HEADS * GDN_HEAD_DIM
CONV_K_QKV = 4
GDN_CHUNK = CHUNK
PROJ_COLS = 3 * CONV_CH + 3 * GDN_W + GDN_W + 2 * GDN_HEADS
SPLIT_AT = [CONV_CH, 2 * CONV_CH, 3 * CONV_CH, 3 * CONV_CH + 3 * GDN_W,
            3 * CONV_CH + 4 * GDN_W, 3 * CONV_CH + 4 * GDN_W + GDN_HEADS]
N_GROUPS = 4
EXPERTS_PER_GROUP = 8
N_EXPERTS = N_GROUPS * EXPERTS_PER_GROUP
TOP_K = 2
D_EXPERT = D_MODEL // 2
EXPERT_BLOCK = 128

kernel_name = "hymba_conv_gdn_hmoe_layer"

def rms_norm(x, w):
    xf = x.astype(jnp.float32)
    y = xf * lax.rsqrt(jnp.mean(xf * xf, axis=-1, keepdims=True) + EPS)
    return (y * w.astype(jnp.float32)).astype(x.dtype)

def l2_normalize(x):
    xf = x.astype(jnp.float32)
    return xf * lax.rsqrt(jnp.sum(xf * xf, axis=-1, keepdims=True) + EPS)

def causal_depthwise_conv(x, w):
    K = w.shape[0]
    L = x.shape[1]
    xp = jnp.pad(x, ((0, 0), (K - 1, 0), (0, 0)))
    acc = xp[:, 0:L] * w[0]
    for j in range(1, K):
        acc = acc + xp[:, j:j + L] * w[j]
    return acc

def gated_delta_rule(q, k, v, g, beta):
    B, H, L, DK = q.shape
    DV = v.shape[-1]
    n_chunks = L // GDN_CHUNK

    def blocks(t):
        return t.reshape(B, H, n_chunks, GDN_CHUNK, *t.shape[3:])

    q, k, v, g, beta = (blocks(t) for t in (q * (DK ** -0.5), k, v, g, beta))
    g = jnp.cumsum(g, axis=-1)
    idx = jnp.arange(GDN_CHUNK)
    incl = idx[:, None] >= idx[None, :]
    strict = idx[:, None] > idx[None, :]
    decay = jnp.exp(jnp.where(incl, g[..., :, None] - g[..., None, :], -jnp.inf))
    kb = k * beta[..., None]
    lower = jnp.where(strict, jnp.einsum('bhnid,bhnjd->bhnij', kb, k) * decay, 0.0)
    eye = jnp.eye(GDN_CHUNK, dtype=q.dtype)
    rhs = jnp.concatenate([v * beta[..., None], kb * jnp.exp(g)[..., None]], axis=-1)
    sol = lax.linalg.triangular_solve(lower + eye, rhs, left_side=True, lower=True,
                                      unit_diagonal=True)
    u, w = sol[..., :DV], sol[..., DV:]
    intra = jnp.einsum('bhnid,bhnjd->bhnij', q, k) * decay
    g_last = g[..., -1]
    qg = q * jnp.exp(g)[..., None]
    kd = k * jnp.exp(g_last[..., None] - g)[..., None]
    a_last = jnp.exp(g_last)
    xs = tuple(jnp.moveaxis(t, 2, 0) for t in (qg, kd, u, w, intra, a_last))

    def step(S, inp):
        qg_c, kd_c, u_c, w_c, intra_c, a_c = inp
        v_new = u_c - jnp.einsum('bhik,bhkv->bhiv', w_c, S)
        o_c = (jnp.einsum('bhik,bhkv->bhiv', qg_c, S)
               + jnp.einsum('bhij,bhjv->bhiv', intra_c, v_new))
        S = S * a_c[..., None, None] + jnp.einsum('bhik,bhiv->bhkv', kd_c, v_new)
        return S, o_c

    S0 = jnp.zeros((B, H, DK, DV), q.dtype)
    _, o = lax.scan(step, S0, xs)
    return jnp.moveaxis(o, 0, 2).reshape(B, H, L, DV)

def hybrid_mixer(xn, w_in, conv_mix_w, conv_mix_norm_w, qkv_conv_w, a_log, dt_bias,
                 gdn_norm_w, w_out):
    B, L, _ = xn.shape
    proj = xn @ w_in
    gate_b, gate_c, u, qkv, z, a, b = jnp.split(proj, SPLIT_AT, axis=-1)

    y_a = gate_b * causal_depthwise_conv(gate_c * u, conv_mix_w)
    y_a = rms_norm(y_a.reshape(B, L, CONV_GROUPS, CONV_CH // CONV_GROUPS),
                   conv_mix_norm_w.reshape(CONV_GROUPS, CONV_CH // CONV_GROUPS))
    y_a = y_a.reshape(B, L, CONV_CH)

    qkv = jax.nn.silu(causal_depthwise_conv(qkv, qkv_conv_w))
    q, k, v = jnp.split(qkv, 3, axis=-1)
    q = l2_normalize(q.reshape(B, L, GDN_HEADS, GDN_HEAD_DIM))
    k = l2_normalize(k.reshape(B, L, GDN_HEADS, GDN_HEAD_DIM))
    v = v.reshape(B, L, GDN_HEADS, GDN_HEAD_DIM).astype(jnp.float32)
    beta = jax.nn.sigmoid(b.astype(jnp.float32))
    g = -jnp.exp(a_log.astype(jnp.float32)) * jax.nn.softplus(
        a.astype(jnp.float32) + dt_bias.astype(jnp.float32))
    pad = (-L) % GDN_CHUNK
    to_bhl = lambda t: jnp.pad(jnp.swapaxes(t, 1, 2),
                               [(0, 0), (0, 0), (0, pad)] + [(0, 0)] * (t.ndim - 3))
    o = gated_delta_rule(to_bhl(q), to_bhl(k), to_bhl(v), to_bhl(g), to_bhl(beta))
    o = jnp.swapaxes(o[:, :, :L], 1, 2).astype(xn.dtype)
    o = rms_norm(o, gdn_norm_w) * jax.nn.silu(z.reshape(B, L, GDN_HEADS, GDN_HEAD_DIM))
    y_b = o.reshape(B, L, GDN_W)

    return jnp.concatenate([y_a, y_b], axis=-1) @ w_out

def grouped_expert_ffn(xf, expert_idx, expert_w, w_gate, w_up, w_down):
    T, D = xf.shape
    n_assign = T * TOP_K
    n_blocks = (n_assign + N_EXPERTS * (EXPERT_BLOCK - 1) + EXPERT_BLOCK - 1) // EXPERT_BLOCK
    n_rows = n_blocks * EXPERT_BLOCK
    flat_e = expert_idx.reshape(-1).astype(jnp.int32)
    flat_w = expert_w.reshape(-1)
    flat_tok = jnp.arange(n_assign, dtype=jnp.int32) // TOP_K
    order = jnp.argsort(flat_e)
    sorted_e = flat_e[order]
    counts = jnp.bincount(flat_e, length=N_EXPERTS).astype(jnp.int32)
    padded = (counts + EXPERT_BLOCK - 1) // EXPERT_BLOCK * EXPERT_BLOCK
    pad_end = jnp.cumsum(padded)
    pad_start = pad_end - padded
    start = jnp.cumsum(counts) - counts
    dest = pad_start[sorted_e] + jnp.arange(n_assign, dtype=jnp.int32) - start[sorted_e]
    row_tok = jnp.full((n_rows,), T, jnp.int32).at[dest].set(flat_tok[order])
    row_w = jnp.zeros((n_rows,), xf.dtype).at[dest].set(flat_w[order].astype(xf.dtype))
    block_start = jnp.arange(n_blocks, dtype=jnp.int32) * EXPERT_BLOCK
    block_expert = jnp.minimum(jnp.searchsorted(pad_end, block_start, side='right'),
                               N_EXPERTS - 1).astype(jnp.int32)
    x_rows = jnp.concatenate([xf, jnp.zeros((1, D), xf.dtype)], axis=0)[row_tok]
    x_rows = x_rows.reshape(n_blocks, EXPERT_BLOCK, D)

    def expert_block(args):
        xb, e = args
        hid = jax.nn.silu(xb @ w_gate[e]) * (xb @ w_up[e])
        return hid @ w_down[e]

    y_rows = lax.map(expert_block, (x_rows, block_expert)).reshape(n_rows, D)
    out = jnp.zeros((T + 1, D), xf.dtype).at[row_tok].add(y_rows * row_w[:, None])
    return out[:T]

def hierarchical_moe(xn, w_group, b_group, w_router, b_router, w_gate, w_up, w_down):
    B, L, D = xn.shape
    xf = xn.reshape(-1, D)
    xr = xf.astype(jnp.float32)
    grp_prob = jax.nn.softmax(xr @ w_group.astype(jnp.float32) + b_group, axis=-1)
    p_grp, g_sel = lax.top_k(grp_prob, 1)
    exp_logits = jnp.einsum('td,dge->tge', xr, w_router.astype(jnp.float32)) + b_router
    exp_logits = jnp.take_along_axis(exp_logits, g_sel[:, :, None], axis=1)[:, 0]
    w_top, e_top = lax.top_k(jax.nn.softmax(exp_logits, axis=-1), TOP_K)
    w_top = w_top / jnp.sum(w_top, axis=-1, keepdims=True) * p_grp
    expert_idx = g_sel * EXPERTS_PER_GROUP + e_top
    y = grouped_expert_ffn(xf, expert_idx, w_top, w_gate, w_up, w_down)
    return y.reshape(B, L, D)

def setup_inputs(seed: int = 0) -> dict:
    key = jax.random.key(seed)
    ks = jax.random.split(key, 24)
    f32 = jnp.float32
    nrm = lambda k, shape, scale: jax.random.normal(k, shape, f32) * scale
    gain = lambda k, shape: 1.0 + 0.02 * jax.random.normal(k, shape, f32)
    dt = jnp.exp(jax.random.uniform(ks[8], (DEPTH, GDN_HEADS), f32,
                                    math.log(1e-3), math.log(1e-1)))
    dt_bias = dt + jnp.log(-jnp.expm1(-dt))
    a_log = jnp.log(jax.random.uniform(ks[7], (DEPTH, GDN_HEADS), f32, 1.0, 16.0))
    return {
        'x': jax.random.normal(ks[0], (BATCH, SEQ, D_MODEL), f32),
        'meta_tokens': nrm(ks[1], (N_META, D_MODEL), 1.0),
        'mix_norm_w': gain(ks[2], (DEPTH, D_MODEL)),
        'w_in': nrm(ks[3], (DEPTH, D_MODEL, PROJ_COLS), D_MODEL ** -0.5),
        'conv_mix_w': nrm(ks[4], (DEPTH, CONV_K_MIX, CONV_CH), CONV_K_MIX ** -0.5),
        'conv_mix_norm_w': gain(ks[5], (DEPTH, CONV_CH)),
        'qkv_conv_w': nrm(ks[6], (DEPTH, CONV_K_QKV, 3 * GDN_W), CONV_K_QKV ** -0.5),
        'a_log': a_log,
        'dt_bias': dt_bias,
        'gdn_norm_w': gain(ks[9], (DEPTH, GDN_HEAD_DIM)),
        'w_out': nrm(ks[10], (DEPTH, D_MIX, D_MODEL), D_MIX ** -0.5),
        'ffn_norm_w': gain(ks[11], (DEPTH, D_MODEL)),
        'w_group': nrm(ks[12], (DEPTH, D_MODEL, N_GROUPS), D_MODEL ** -0.5),
        'b_group': nrm(ks[13], (DEPTH, N_GROUPS), 0.01),
        'w_router': nrm(ks[14], (DEPTH, D_MODEL, N_GROUPS, EXPERTS_PER_GROUP), D_MODEL ** -0.5),
        'b_router': nrm(ks[15], (DEPTH, N_GROUPS, EXPERTS_PER_GROUP), 0.01),
        'w_gate': nrm(ks[16], (DEPTH, N_EXPERTS, D_MODEL, D_EXPERT), D_MODEL ** -0.5),
        'w_up': nrm(ks[17], (DEPTH, N_EXPERTS, D_MODEL, D_EXPERT), D_MODEL ** -0.5),
        'w_down': nrm(ks[18], (DEPTH, N_EXPERTS, D_EXPERT, D_MODEL), D_EXPERT ** -0.5),
        'final_norm_w': gain(ks[19], (D_MODEL,)),
    }

def reference(x, meta_tokens, mix_norm_w, w_in, conv_mix_w, conv_mix_norm_w, qkv_conv_w,
              a_log, dt_bias, gdn_norm_w, w_out, ffn_norm_w, w_group, b_group, w_router,
              b_router, w_gate, w_up, w_down, final_norm_w):
    B = x.shape[0]
    meta = jnp.broadcast_to(meta_tokens.astype(x.dtype)[None], (B, N_META, D_MODEL))
    h = jnp.concatenate([meta, x], axis=1)
    for layer in range(DEPTH):
        xn = rms_norm(h, mix_norm_w[layer])
        h = h + hybrid_mixer(xn, w_in[layer], conv_mix_w[layer], conv_mix_norm_w[layer],
                             qkv_conv_w[layer], a_log[layer], dt_bias[layer],
                             gdn_norm_w[layer], w_out[layer])
        xn = rms_norm(h, ffn_norm_w[layer])
        h = h + hierarchical_moe(xn, w_group[layer], b_group[layer], w_router[layer],
                                 b_router[layer], w_gate[layer], w_up[layer], w_down[layer])
    out = rms_norm(h, final_norm_w)
    return out[:, N_META:]


_drawn_inputs = setup_inputs


def setup_inputs(seed=0):
    import zlib

    import numpy as np

    out = dict(_drawn_inputs(seed))
    spreads = {}
    factors = {'conv_mix_norm_w': 8.118,
     'gdn_norm_w': 12.555,
     'b_group': 33.129,
     'b_router': 25.236,
     'final_norm_w': 8.064,
     'ffn_norm_w': 4.712}
    for name, (base, spread) in spreads.items():
        noise = np.random.default_rng([zlib.crc32(name.encode()), seed]).standard_normal(out[name].shape)
        drawn = base * np.exp(spread * noise) if base else spread * noise
        out[name] = jnp.asarray(drawn.astype(out[name].dtype))
    for name, factor in factors.items():
        out[name] = (out[name] * factor).astype(out[name].dtype)
    return out
```

```python
from contextlib import ExitStack

import numpy as np

import concourse.bass as bass
from concourse import mybir

F32 = mybir.dt.float32
I32 = mybir.dt.int32
ALU = mybir.AluOpType
ACT = mybir.ActivationFunctionType
AX_X = mybir.AxisListType.X

D = 1024
META = 16
L = META + 1024
KD = D // 128
C = 104
NC = L // C
H = 4
KINDS = 7
Z, GC, UU, GB, Q, K, V = range(KINDS)
PIECE = [(0, 347), (347, 347), (694, 346)]
LEVELS = 7
GROUPS = [range(0, 4), range(4, 8), range(8, 10)]
E = 32
NG = 4
EPG = E // NG
CAP = 128
OVER = (2 * L - 1) // CAP
BLOCKS = E + OVER
MAXQ = -(-L // CAP) - 1
BIG = 4096
FE = 512
GRP_DIFF, TOP_DIFF, RANK_IN, TABLE_IN = 6, 27, 51, 101
EPS = 1e-6
STOP = None
WU = 4096
NCOL = 28 * 1024

CONST = {}
_at = 0
for _n, _w in [("ident", 128), ("ones", 128), ("bones", 128), ("incl", C), ("strict", C), ("lev", LEVELS * C),
               ("iota", 128), ("tok", NC), ("dst", 2 * NC), ("r4", NG), ("r8", EPG), ("eps", 1), ("qb", 1)]:
    CONST[_n] = (_at, _w)
    _at += _w
NCONST = _at
PAR = {}
_at = 0
for _n, _w in [("taps", 5 * 16), ("mixw", KD), ("gw", 1), ("wab", KD * 8), ("wr", KD * 36), ("bias", 36),
               ("alog", H), ("dt", H)]:
    PAR[_n] = (_at, _w)
    _at += _w
NPAR = _at


def constants():
    a = np.zeros((128, NCONST), np.float32)

    def put(name, v):
        o, w = CONST[name]
        a[: v.shape[0], o:o + w] = v

    i = np.arange(128)
    c = np.arange(C)
    put("ident", np.eye(128))
    put("ones", np.ones((128, 128)))
    put("bones", (i[:, None] // 64 == i[None, :] // 64) * 1.0)
    put("incl", (c[None, :] >= c[:, None]) * 1.0)
    put("strict", (c[None, :] > c[:, None]) * 1.0)
    lev = []
    for n in range(LEVELS):
        s = 1 << n
        r, q = c[:, None], c[None, :]
        lev.append((r // (2 * s) == q // (2 * s)) & ((r // s) % 2 == 1) & ((q // s) % 2 == 0))
    put("lev", np.concatenate(lev, 1) * 1.0)
    put("iota", np.broadcast_to(i[None, :], (128, 128)))
    tok = i[:C, None] + C * np.arange(NC)[None, :]
    put("tok", tok - BIG)
    put("dst", (2 * tok[:, :, None] + np.arange(2)[None, None, :] - BIG).reshape(C, 2 * NC))
    put("r4", np.broadcast_to(8 - np.arange(NG)[None, :], (128, NG)))
    put("r8", np.broadcast_to(16 - np.arange(EPG)[None, :], (128, EPG)))
    put("eps", np.full((128, 1), EPS))
    put("qb", np.full((128, 1), -0.5 * np.log(128.0)))
    return a


def layer_kernel(nc, x, consts, par, wt, w_out, ffn_w, fin_w, w_gate, w_up, w_down, out, stop=None):
    ctx = ExitStack()
    with ctx:
        NF = 52900
        arena = ctx.enter_context(nc.sbuf_tensor("arena", [128, NF], F32))
        bank = [ctx.enter_context(nc.psum_tensor(f"bank{i}", [128, 512], F32)) for i in range(8)]
        h_dram = nc.dram_tensor("h_rows", (L, D), F32, kind="Internal").ap()
        xn_dram = nc.dram_tensor("xn_rows", (L, D), F32, kind="Internal").ap()
        y_dram = nc.dram_tensor("y_rows", (2 * L, D), F32, kind="Internal").ap()

        def sem(name):
            return ctx.enter_context(nc.semaphore(name))

        class Zone:
            def __init__(self, at, end):
                self.at, self.end = at, end

            def take(self, *dims):
                n = int(np.prod(dims))
                a = arena[:, self.at:self.at + n]
                self.at += n
                assert self.at <= self.end, (self.at, self.end)
                if len(dims) == 2:
                    a = a.rearrange("p (a b) -> p a b", a=dims[0])
                if len(dims) == 3:
                    a = a.rearrange("p (a b c) -> p a b c", a=dims[0], b=dims[1])
                return a

        keep = Zone(0, 3540)
        zy = Zone(3540, 3540 + 8320)
        zx = Zone(zy.end, zy.end + 8320)
        GBASE = zx.end
        zg = Zone(GBASE, NF)

        const_sb = keep.take(NCONST)
        par_sb = keep.take(NPAR)

        def const(name, rows=128):
            o, w = CONST[name]
            return const_sb[0:rows, o:o + w]

        def param(name, rows=128):
            o, w = PAR[name]
            return par_sb[0:rows, o:o + w]

        ident, ones, bones = const("ident"), const("ones"), const("bones")
        incl, strict = const("incl", C), const("strict", C)
        lev = const("lev", C).rearrange("p (l j) -> p l j", l=LEVELS)
        eps = const("eps")
        taps_all = param("taps")
        mixw, gw = param("mixw"), param("gw")
        wab = param("wab").rearrange("p (k n) -> p k n", k=KD)
        wr = param("wr").rearrange("p (k n) -> p k n", k=KD)
        tok_sc = keep.take(H, 4, NC)
        a_last = keep.take(H, NC)
        g_tok = keep.take(H, NC)
        head_sc = keep.take(4, NC)
        head_a = keep.take(NC)
        taps = keep.take(16)
        state = keep.take(128)
        small = keep.take(4, 40)
        stat = keep.take(2, 4)
        ea = keep.take(H)
        logits = keep.take(NC, 36)
        itab = keep.take(BLOCKS, 2).bitcast(I32)
        wtab = keep.take(BLOCKS)
        over_i = keep.take(OVER + 1).bitcast(I32)

        yT = zy.take(2 * H, L)
        xnT = zx.take(KD, L)
        raw = [zg.take(1044), zg.take(1044)]
        cv = [zg.take(L) for _ in range(3)]
        sq = [zg.take(L), zg.take(L)]
        rs = [zg.take(L), zg.take(L)]
        qT, kT, vT = zg.take(L), zg.take(L), zg.take(L)
        zs = zg.take(L)
        oT = zg.take(L)
        eG = zg.take(L)
        qg = zg.take(L)
        wst = [zg.take(KD, 128) for _ in range(4)]
        r_sb, vn_sb = zg.take(128), zg.take(128)
        x_at = zg.at
        gbc = zg.take(NC, 128)
        bv = zg.take(NC, 128)
        kd = zg.take(NC, 128)
        dT = zg.take(NC, C)
        dTi = zg.take(NC, C)
        dTs = zg.take(NC, C)
        mT = zg.take(NC, C)
        aL = [zg.take(NC, C), zg.take(NC, C)]
        rT = zg.take(NC, C)
        tI = dT
        zz = dTs
        lM = mT
        zn = Zone(x_at, NF)
        x_sb = [zn.take(D), zn.take(D)]
        xn_sb = [zn.take(D), zn.take(D)]
        junk = zn.take(D)

        wexp = [arena[:, GBASE + i * WU:GBASE + (i + 1) * WU] for i in range(6)]
        zo = Zone(GBASE + 6 * WU, NF)
        h_sb = [zo.take(D), zo.take(D)]
        x2_sb = [zo.take(D), zo.take(D)]
        y_st = [zo.take(KD, C), zo.take(KD, C)]
        x2T = zo.take(KD, C)
        ffw = zo.take(D)
        wo_sb = xnT.rearrange("p k l -> p (k l)")[:, 0:KD * D].rearrange("p (k n) -> p k n", k=KD)

        s_const, s_wout, s_ffw = sem("const_loaded"), sem("w_out_loaded"), sem("ffw_loaded")
        x_loaded = [sem("x_loaded0"), sem("x_loaded1")]
        ss_done, rstd_done = sem("ss_done"), sem("rstd_done")
        xn_done, xt_done, xnT_done = sem("xn_done"), sem("xt_done"), sem("xnT_done")
        zeros_done = sem("zeros_done")
        ab_done, gt_done, gates_dve, gates_act, gsum_done = (sem("ab_done"), sem("g_tok_done"), sem("gates_dve"),
                                                             sem("gates_act"), sem("gsum_done"))
        w_loaded = [sem(f"w_loaded{i}") for i in range(4)]
        proj_done, proj_act, proj_dve = sem("proj_done"), sem("proj_act"), sem("proj_dve")
        head_done = sem("head_done")
        gdn_done, gdn_act, gdn_dve = sem("gdn_done"), sem("gdn_act"), sem("gdn_dve")
        dt_sub, dexp_done = sem("dt_sub"), sem("dexp_done")
        dti_done, dts_done, qg_done = sem("dti_done"), sem("dts_done"), sem("qg_done")
        a_done, t0_done = sem("a_done"), sem("t0_done")
        mixy_done, silu_done, sq_done = sem("mixy_done"), sem("silu_done"), sem("sq_done")
        taps_done, adt_done = sem("taps_done"), sem("adt_done")
        conv_step = sem("conv_step")
        sum_done, sum_act, rs_done = sem("sum_done"), sem("sum_act"), sem("rs_done")
        qk_done, oy_part, oy_done = sem("qk_done"), sem("oy_part"), sem("oy_done")
        s_done, ks_done, r_done = sem("state_done"), sem("ks_done"), sem("r_done")
        vnp_done, vn_done, ods_done, o_done = sem("vnp_done"), sem("vn_done"), sem("ods_done"), sem("o_done")

        yst_done, out_done, res_done, x2_done = sem("yst_done"), sem("out_done"), sem("res_done"), sem("x2_done")
        xr_loaded = [sem("xr_loaded0"), sem("xr_loaded1")]
        h_stored, x2_stored = sem("h_stored"), sem("x2_stored")
        ff_stat, ffr_done, tr_done, x2T_done = sem("ff_stat"), sem("ffr_done"), sem("tr_done"), sem("x2T_done")
        lg_ps, lg_done = sem("logits_in_psum"), sem("logits_done")
        w_sem = [sem(f"expert_w_loaded{i}") for i in range(6)]

        zr = Zone(zy.end - 8320, zy.end)
        slot1h = zr.take(2 * NC, 128)
        blk1h = zr.take(2 * NC, BLOCKS)
        e1h = [zr.take(NC, E), zr.take(NC, E)]
        ecnt, epre = zr.take(NC, E), zr.take(NC, E)
        e3 = zr.take(NC, E)
        nover, oend, obase, tcnt = zr.take(E), zr.take(E), zr.take(E), zr.take(E)
        grp_v = [zr.take(NC, NG) for _ in range(3)]
        exp_v = [zr.take(NC, EPG) for _ in range(6)]
        tk = [zr.take(NC) for _ in range(8)]
        tk2 = [zr.take(2 * NC) for _ in range(8)]
        ocmp = zr.take(OVER, E)
        ofl = zr.take(OVER + 1)
        ttab = zr.take(BLOCKS, 2)
        zv = Zone(NF - 3 * 2 * NC * BLOCKS, NF)
        vals = zv.take(2 * NC, 3, BLOCKS)

        ze = Zone(zy.end, zy.end + 8320)
        xg = [ze.take(D), ze.take(D)]
        xgT = [ze.take(KD, 128), ze.take(KD, 128)]
        gs = [ze.take(FE), ze.take(FE)]
        hid = ze.take(FE)
        hidT = ze.take(4, 128)
        ysb = [x2_sb[0], x2_sb[1]]
        gi = [ze.take(1).bitcast(I32) for _ in range(2)]
        si = [ze.take(1).bitcast(I32) for _ in range(2)]
        wcol = [ze.take(1) for _ in range(2)]

        r_dve, r_act, r_pe, tables = sem("route_dve"), sem("route_act"), sem("route_pe"), sem("tables_done")
        xg_zero, icol, gathered, scattered = sem("xg_zero"), sem("icol_done"), [sem("gathered0"), sem("gathered1")], sem("scattered")
        xt_e, xte_act, xte_dve = sem("xt_experts"), sem("xte_act"), sem("xte_dve")
        g_done, u_done, silu_e, hid_done = sem("gate_done"), sem("up_done"), sem("silu_e"), sem("hid_done")
        ht_e, hte_done, d_done, y_act, y_dve = sem("ht_experts"), sem("hte_done"), sem("down_done"), sem("y_act"), sem("y_dve")
        moe_done, gi2_done = sem("moe_done"), sem("gi2_done")
        hf_loaded, yf_loaded = [sem("hf_loaded0"), sem("hf_loaded1")], [sem("yf_loaded0"), sem("yf_loaded1")]
        fw_loaded = sem("fw_loaded")
        f_sum, f_add, f_stat, f_rstd, f_out = sem("f_sum"), sem("f_add"), sem("f_stat"), sem("f_rstd"), sem("f_out")
        f_stored = [sem("f_stored0"), sem("f_stored1")]

        FT = (L - META) // 128
        zf = Zone(zy.end - 8320, zy.end)
        hf = [zf.take(D), zf.take(D)]
        yf = [zf.take(2 * D), zf.take(2 * D)]
        of = [zf.take(D), zf.take(D)]
        fw = h_sb[0]

        UNIT_SRC = [w_gate, w_up, w_down]

        def load_unit(eng, e, slot):
            src = UNIT_SRC[slot % 3]
            kk = KD if slot % 3 < 2 else FE // 128
            if isinstance(e, int):
                s = src[e].rearrange("(k p) n -> p k n", p=128)
            else:
                s = src[bass.ds(e, 1)].rearrange("o (k p) n -> (o p) k n", p=128)
            eng.dma_start(wexp[slot].rearrange("p (k n) -> p k n", k=kk), s).then_inc(w_sem[slot], 16)

        def over_loop(eng, body):
            total = eng.value_load(over_i[0:1, OVER:OVER + 1], min_val=0, max_val=OVER)
            with eng.Fori(0, OVER) as j:
                with eng.If(j < total):
                    body(j)

        def tail_sync(sp):
            sp.wait_ge(oy_done, H)
            sp.dma_start(ffw, ffn_w).then_inc(s_ffw, 16)
            for u in range(2):
                sp.dma_start(h_sb[u][0:C, :], x[u * C:(u + 1) * C, :]).then_inc(xr_loaded[u], 16)

            def store(i, u, t):
                rows = slice(t * C, (t + 1) * C) if isinstance(t, int) else bass.ds(t * C, C)
                sp.wait_ge(res_done, (t + 1) * 2)
                sp.dma_start(h_dram[rows, :], h_sb[u][0:C, :]).then_inc(h_stored, 16)
                sp.wait_ge(x2_done, t + 1)
                sp.dma_start(xn_dram[rows, :], x2_sb[u][0:C, :]).then_inc(x2_stored, 16)
                sp.wait_ge(h_stored, (t + 1) * 16)
                sp.wait_ge(x2_stored, (t + 1) * 16)

            with sp.Fori(0, NC // 2 - 1) as i:
                for u in range(2):
                    store(i, u, i * 2 + u)
                    sp.dma_start(h_sb[u][0:C, :], x[bass.ds((i * 2 + u + 2) * C, C), :]).then_inc(xr_loaded[u], 16)
            for u in range(2):
                store(None, u, NC - 2 + u)
            sp.wait_ge(tables, 1)
            sp.dma_start(fw, fin_w).then_inc(fw_loaded, 16)
            if stop == "route":
                sp.wait_ge(fw_loaded, 16)
                for s in range(6):
                    sp.wait_ge(w_sem[s], 16)
                return
            sp.wait_ge(g_done, 1)
            load_unit(sp, 2, 0)
            sp.wait_ge(u_done, 1)
            load_unit(sp, 2, 1)

            def refill(e, p):
                sp.wait_ge(g_done, e + 1)
                load_unit(sp, e + 2, 3 * p)
                sp.wait_ge(d_done, e)
                load_unit(sp, e + 1, 3 * (1 - p) + 2)
                sp.wait_ge(u_done, e + 1)
                load_unit(sp, e + 2, 3 * p + 1)

            with sp.Fori(0, (E - 4) // 2) as j:
                refill(j * 2 + 1, 1)
                refill(j * 2 + 2, 0)
            refill(E - 3, 1)
            sp.wait_ge(d_done, E - 2)
            load_unit(sp, E - 1, 5)

            def over(j):
                ex = sp.value_load(over_i[0:1, bass.ds(j, 1)], min_val=0, max_val=E - 1)
                sp.wait_ge(d_done, j + E)
                for s in range(3):
                    load_unit(sp, ex, s)

            over_loop(sp, over)
            sp.wait_ge(moe_done, 1)
            h_v, y_v = h_dram, y_dram.rearrange("(t k) d -> t (k d)", k=2)

            def fetch(u, t):
                rows = slice(META + t * 128, META + (t + 1) * 128) if isinstance(t, int) else bass.ds(t * 128 + META, 128)
                sp.dma_start(hf[u], h_v[rows, :]).then_inc(hf_loaded[u], 16)
                sp.dma_start(yf[u], y_v[rows, :]).then_inc(yf_loaded[u], 16)

            def put(u, t):
                rows = slice(t * 128, (t + 1) * 128) if isinstance(t, int) else bass.ds(t * 128, 128)
                sp.wait_ge(f_out, t + 1)
                sp.dma_start(out[rows, :], of[u]).then_inc(f_stored[u], 16)

            for u in range(2):
                fetch(u, u)
            with sp.Fori(0, FT // 2 - 1) as i:
                for u in range(2):
                    put(u, i * 2 + u)
                    sp.wait_ge(f_stored[u], i * 16 + 16)
                    fetch(u, i * 2 + u + 2)
            for u in range(2):
                put(u, FT - 2 + u)
            for u in range(2):
                sp.wait_ge(f_stored[u], 16 * FT // 2)

        def tail_tensor(pe):
            pe.wait_ge(s_wout, 16)

            def out_proj(t, u):
                pe.wait_ge(yst_done, t + 1)
                for b in range(2):
                    for k in range(KD):
                        m = nc.tensor.matmul(bank[2 * u + b][0:C, :], y_st[u][:, k, :], wo_sb[:, k, b * 512:(b + 1) * 512],
                                             start=(k == 0), stop=(k == KD - 1))
                    m.then_inc(out_done, 1)

            def router(t, u):
                pe.wait_ge(x2_done, t + 1)
                for b in range(2):
                    for k in range(4):
                        m = nc.tensor.transpose(bank[4 + b][:, k * C:(k + 1) * C],
                                                x2_sb[u][0:C, (4 * b + k) * 128:(4 * b + k + 1) * 128], ident[0:C, 0:C])
                    m.then_inc(tr_done, 1)
                pe.wait_ge(x2T_done, (t + 1) * 2)
                for k in range(KD):
                    m = nc.tensor.matmul(bank[6 + u][0:C, 0:36], x2T[:, k, :], wr[:, k, :], start=(k == 0), stop=(k == KD - 1))
                m.then_inc(lg_ps, 1)

            out_proj(0, 0)
            with pe.Fori(0, NC // 2 - 1) as i:
                out_proj(i * 2 + 1, 1)
                router(i * 2, 0)
                out_proj(i * 2 + 2, 0)
                router(i * 2 + 1, 1)
            out_proj(NC - 1, 1)
            router(NC - 2, 0)
            router(NC - 1, 1)
            pe.wait_ge(r_dve, RANK_IN)
            flat = lambda a: a[0:C].rearrange("p t e -> p (t e)")
            nc.tensor.matmul(bank[0][0:C, 0:NC * E], strict, flat(ecnt), start=True, stop=False)
            nc.tensor.matmul(bank[0][0:C, 0:NC * E], ones[0:C, 0:C], flat(epre), start=False, stop=True)
            nc.tensor.matmul(bank[1][:, 0:E], ones[0:C, :], tcnt[0:C], start=True, stop=True).then_inc(r_pe, 1)
            pe.wait_ge(r_dve, TABLE_IN)
            for n in range(2 * NC):
                m = nc.tensor.matmul(bank[2][:, 0:3 * BLOCKS], slot1h[0:C, n, :],
                                     vals[0:C, n].rearrange("p a b -> p (a b)"), start=(n == 0), stop=(n == 2 * NC - 1))
            m.then_inc(r_pe, 1)
            if stop == "route":
                return

            def turn(e, p, loads):
                pe.wait_ge(gathered[p], loads)
                for b in range(2):
                    for k in range(4):
                        m = nc.tensor.transpose(bank[5 + b][:, k * 128:(k + 1) * 128],
                                                xg[p][:, (4 * b + k) * 128:(4 * b + k + 1) * 128], ident)
                m.then_inc(xt_e, 1)

            def in_proj(e, p, slot, loads):
                pe.wait_ge(w_sem[slot], loads)
                if slot % 3 == 0:
                    pe.wait_ge(xte_act, e + 1)
                    pe.wait_ge(xte_dve, e + 1)
                w = wexp[slot].rearrange("p (k n) -> p k n", k=KD)
                b = p if slot % 3 == 0 else 2
                for k in range(KD):
                    m = nc.tensor.matmul(bank[b][:, :], xgT[p][:, k, :], w[:, k, :], start=(k == 0), stop=(k == KD - 1))
                m.then_inc(g_done if slot % 3 == 0 else u_done, 1)

            def down(e, slot, loads):
                pe.wait_ge(hid_done, e + 1)
                for k in range(4):
                    m = nc.tensor.transpose(bank[7][:, k * 128:(k + 1) * 128], hid[:, k * 128:(k + 1) * 128], ident)
                m.then_inc(ht_e, 1)
                pe.wait_ge(w_sem[slot], loads)
                pe.wait_ge(hte_done, e + 1)
                w = wexp[slot].rearrange("p (k n) -> p k n", k=4)
                for b in range(2):
                    for k in range(4):
                        m = nc.tensor.matmul(bank[3 + b][:, :], hidT[:, k, :], w[:, k, b * 512:(b + 1) * 512],
                                             start=(k == 0), stop=(k == 3))
                m.then_inc(d_done, 1)

            turn(0, 0, 16)
            in_proj(0, 0, 0, 16)
            turn(1, 1, 16)
            in_proj(0, 0, 1, 16)

            def expert(e, p, n):
                in_proj(e, p, 3 * p, n * 16 + 16)
                down(e - 1, 3 * (1 - p) + 2, (n + (1 if p else 0)) * 16)
                turn(e + 1, 1 - p, (n + (1 if p else 0)) * 16 + 16)
                in_proj(e, p, 3 * p + 1, n * 16 + 16)

            with pe.Fori(0, E // 2 - 1) as j:
                expert(j * 2 + 1, 1, j)
                expert(j * 2 + 2, 0, j + 1)
            n = E // 2 - 1
            in_proj(E - 1, 1, 3, n * 16 + 16)
            down(E - 2, 2, n * 16 + 16)
            in_proj(E - 1, 1, 4, n * 16 + 16)
            down(E - 1, 5, n * 16 + 16)

            def over(j):
                loads = j * 16 + 16 * (E // 2 + 1)
                turn(j + E, 0, loads)
                in_proj(j + E, 0, 0, loads)
                in_proj(j + E, 0, 1, loads)
                down(j + E, 2, loads)

            over_loop(pe, over)

        def tail_scalar(act):
            act.wait_ge(oy_done, H)
            for s in range(6):
                load_unit(act, s // 3, s)

            def chunk_ff(i, u, t):
                act.wait_ge(res_done, (t + 1) * 2)
                nc.scalar.activation(x2_sb[u][0:C, :], h_sb[u][0:C, :], ACT.Square,
                                     accum_out=stat[0:C, u, 0:1]).then_inc(ff_stat, 1)
                act.wait_ge(ff_stat, t * 2 + 1)
                nc.scalar.activation(stat[0:C, u, 1:2], stat[0:C, u, 0:1], ACT.Ln, scale=1.0 / D,
                                     bias=eps[0:C, :]).then_inc(ff_stat, 1)
                act.wait_ge(ff_stat, t * 2 + 2)
                nc.scalar.activation(stat[0:C, u, 2:3], stat[0:C, u, 1:2], ACT.Exp, scale=-0.5).then_inc(ffr_done, 1)
                for b in range(2):
                    act.wait_ge(tr_done, t * 2 + b + 1)
                    nc.scalar.activation(x2T[:, 4 * b:4 * b + 4, :],
                                         bank[4 + b][:, 0:4 * C].rearrange("p (k c) -> p k c", k=4),
                                         ACT.Copy).then_inc(x2T_done, 1)

            with act.Fori(0, NC // 2) as i:
                for u in range(2):
                    chunk_ff(i, u, i * 2 + u)
            act.wait_ge(r_dve, GRP_DIFF)
            nc.scalar.activation(grp_v[1][0:C], grp_v[1][0:C], ACT.Exp).then_inc(r_act, 1)
            act.wait_ge(r_dve, TOP_DIFF)
            nc.scalar.activation(tk[4][0:C], tk[4][0:C], ACT.Exp).then_inc(r_act, 1)
            if stop == "route":
                return

            def turned(e, p):
                act.wait_ge(xt_e, e + 1)
                nc.scalar.activation(xgT[p][:, 0:4, :], bank[5][:, :].rearrange("p (k n) -> p k n", k=4),
                                     ACT.Copy).then_inc(xte_act, 1)

            def silu_gate(e, p):
                act.wait_ge(g_done, e + 1)
                nc.scalar.activation(gs[p], bank[p][:, :], ACT.Silu).then_inc(silu_e, 1)

            def down_in(e):
                act.wait_ge(ht_e, e + 1)
                nc.scalar.activation(hidT, bank[7][:, :].rearrange("p (k n) -> p k n", k=4), ACT.Copy).then_inc(hte_done, 1)

            def y_out(e, p):
                act.wait_ge(d_done, e + 1)
                act.wait_ge(icol, e + 2)
                nc.scalar.activation(ysb[p][:, 0:512], bank[3][:, :], ACT.Copy, scale=wcol[p]).then_inc(y_act, 1)

            turned(0, 0)
            silu_gate(0, 0)
            turned(1, 1)

            def expert(e, p):
                silu_gate(e, p)
                down_in(e - 1)
                y_out(e - 1, 1 - p)
                turned(e + 1, 1 - p)

            with act.Fori(0, E // 2 - 1) as j:
                expert(j * 2 + 1, 1)
                expert(j * 2 + 2, 0)
            silu_gate(E - 1, 1)
            down_in(E - 2)
            y_out(E - 2, 0)
            down_in(E - 1)
            act.wait_ge(scattered, 16 * (E - 2))
            y_out(E - 1, 1)

            def over(j):
                turned(j + E, 0)
                silu_gate(j + E, 0)
                down_in(j + E)
                y_out(j + E, 0)

            over_loop(act, over)
            with act.Fori(0, FT // 2) as i:
                for u in range(2):
                    act.wait_ge(f_add, i * 2 + u + 1)
                    nc.scalar.activation(of[u], hf[u], ACT.Square, accum_out=stat[:, u, 0:1]).then_inc(f_stat, 1)
                    act.wait_ge(f_stat, i * 4 + 2 * u + 1)
                    nc.scalar.activation(stat[:, u, 1:2], stat[:, u, 0:1], ACT.Ln, scale=1.0 / D, bias=eps).then_inc(f_stat, 1)
                    act.wait_ge(f_stat, i * 4 + 2 * u + 2)
                    nc.scalar.activation(stat[:, u, 2:3], stat[:, u, 1:2], ACT.Exp, scale=-0.5).then_inc(f_rstd, 1)

        def tail_vector(dve):
            def logits_of(t, u):
                dve.wait_ge(lg_ps, t + 1)
                o = logits[0:C, t, :] if isinstance(t, int) else logits[0:C, bass.ds(t, 1), :].rearrange("p o n -> p (o n)")
                nc.vector.tensor_tensor(o, bank[6 + u][0:C, 0:36], param("bias", C), ALU.add).then_inc(lg_done, 1)

            dve.wait_ge(s_ffw, 16)
            with dve.Fori(0, NC // 2) as i:
                for u in range(2):
                    t = i * 2 + u
                    dve.wait_ge(xr_loaded[u], i * 16 + 16)
                    for b in range(2):
                        dve.wait_ge(out_done, t * 2 + b + 1)
                        hs = h_sb[u][0:C, b * 512:(b + 1) * 512]
                        nc.vector.tensor_tensor(hs, bank[2 * u + b][0:C, :], hs, ALU.add).then_inc(res_done, 1)
                    dve.wait_ge(ffr_done, t + 1)
                    nc.vector.scalar_tensor_tensor(x2_sb[u][0:C, :], h_sb[u][0:C, :], stat[0:C, u, 2:3], ffw[0:C, :],
                                                   ALU.mult, ALU.mult).then_inc(x2_done, 1)
                    logits_of(t, u)
            dve.wait_ge(lg_done, NC)

            steps = [0]

            def step(ins):
                steps[0] += 1
                ins.then_inc(r_dve, 1)
                dve.wait_ge(r_dve, steps[0])
                return steps[0]

            tt, stt, ts = nc.vector.tensor_tensor, nc.vector.scalar_tensor_tensor, nc.vector.tensor_scalar

            def red(o, i, op):
                return nc.vector.tensor_reduce(o, i, AX_X, op)

            def per(a, n):
                return a.unsqueeze(2).to_broadcast([C, a.shape[1], n])

            def first_max(v, rank_c, best, hot, tmp, n):
                step(red(best, v, ALU.max))
                step(tt(hot, v, per(best, n), ALU.is_equal))
                step(tt(hot, hot, rank_c.unsqueeze(1).to_broadcast([C, NC, n]), ALU.mult))
                step(red(tmp, hot, ALU.max))
                step(tt(hot, hot, per(tmp, n), ALU.is_equal))

            lgt = logits[0:C]
            lg, le = lgt[:, :, 0:NG], lgt[:, :, NG:36].rearrange("p t (g e) -> p t g e", g=NG)
            T = [a[0:C] for a in tk]
            G = [a[0:C] for a in grp_v]
            X = [a[0:C] for a in exp_v]
            first_max(lg, const("r4", C), T[0], G[0], T[1], NG)
            n = step(tt(G[1], lg, per(T[0], NG), ALU.subtract))
            assert n == GRP_DIFF, (n, "GRP_DIFF")
            dve.wait_ge(r_act, 1)
            step(red(T[2], G[1], ALU.add))
            step(nc.vector.reciprocal(T[2], T[2]))
            prod = e3[0:C].rearrange("p t (g e) -> p t g e", g=NG)
            for g in range(NG):
                step(tt(prod[:, :, g, :], le[:, :, g, :], per(G[0][:, :, g], EPG), ALU.mult))
            step(tt(X[0], prod[:, :, 0, :], prod[:, :, 1, :], ALU.add))
            step(tt(X[1], prod[:, :, 2, :], prod[:, :, 3, :], ALU.add))
            step(tt(X[0], X[0], X[1], ALU.add))
            first_max(X[0], const("r8", C), T[3], X[1], T[1], EPG)
            step(stt(X[2], X[1], -1e30, X[0], ALU.mult, ALU.add))
            first_max(X[2], const("r8", C), T[4], X[3], T[1], EPG)
            n = step(tt(T[4], T[4], T[3], ALU.subtract))
            assert n == TOP_DIFF, (n, "TOP_DIFF")
            dve.wait_ge(r_act, 2)
            wk = tk2[0][0:C].rearrange("p (t k) -> p t k", k=2)
            step(ts(T[5], T[4], 1.0, None, ALU.add))
            step(nc.vector.reciprocal(T[5], T[5]))
            step(tt(wk[:, :, 0], T[5], T[2], ALU.mult))
            step(tt(wk[:, :, 1], wk[:, :, 0], T[4], ALU.mult))
            for k in range(2):
                v = e1h[k][0:C].rearrange("p t (g e) -> p t g e", g=NG)
                for g in range(NG):
                    step(tt(v[:, :, g, :], X[1 + 2 * k], per(G[0][:, :, g], EPG), ALU.mult))
            step(tt(ecnt[0:C], e1h[0][0:C], e1h[1][0:C], ALU.add))
            step(nc.vector.memset(epre[0:C, 0, :], 0.0))
            for t in range(1, NC):
                step(tt(epre[0:C, t, :], epre[0:C, t - 1, :], ecnt[0:C, t - 1, :], ALU.add))
            n = step(tt(tcnt[0:C], epre[0:C, NC - 1, :], ecnt[0:C, NC - 1, :], ALU.add))
            assert n == RANK_IN, (n, "RANK_IN")
            dve.wait_ge(r_pe, 1)
            step(nc.vector.tensor_copy(oend, bank[1][:, 0:E]))
            step(ts(nover, oend, float(CAP), None, ALU.is_gt))
            for q in range(2, MAXQ + 1):
                step(stt(nover, oend, float(CAP * q), nover, ALU.is_gt, ALU.add))
            step(nc.vector.memset(tcnt, 1.0))
            step(nc.vector.tensor_tensor_scan(oend, tcnt, nover, 0.0, ALU.mult, ALU.add))
            step(tt(obase, oend, nover, ALU.subtract))
            step(tt(ocmp[0:1], oend[0:1].unsqueeze(1).to_broadcast([1, OVER, E]),
                    const("iota", 1)[:, 0:OVER].unsqueeze(2).to_broadcast([1, OVER, E]), ALU.is_le))
            step(red(ofl[0:1, 0:OVER], ocmp[0:1], ALU.add))
            step(ts(ofl[0:1, 0:OVER], ofl[0:1, 0:OVER], float(E - 1), None, ALU.min))
            step(nc.vector.tensor_copy(ofl[0:1, OVER:OVER + 1], oend[0:1, E - 1:E]))
            step(nc.vector.tensor_copy(over_i[0:1, :], ofl[0:1, :]))
            rk, ex, ob, qq = [tk2[n][0:C].rearrange("p (t k) -> p t k", k=2) for n in (1, 2, 3, 4)]
            ei = const("iota", C)[:, 0:E].unsqueeze(1).to_broadcast([C, NC, E])
            obb = obase[0:C].unsqueeze(1).to_broadcast([C, NC, E])
            rank_ps = bank[0][0:C, 0:NC * E].rearrange("p (t e) -> p t e", e=E)
            for k in range(2):
                for dst, v in ((rk, rank_ps), (ex, ei), (ob, obb)):
                    step(tt(e3[0:C], v, e1h[k][0:C], ALU.mult))
                    step(red(dst[:, :, k], e3[0:C], ALU.add))
            F = [tk2[n][0:C] for n in range(8)]
            step(ts(F[4], F[1], float(CAP), None, ALU.is_ge))
            for q in range(2, MAXQ + 1):
                step(stt(F[4], F[1], float(CAP * q), F[4], ALU.is_ge, ALU.add))
            step(stt(F[5], F[4], -float(CAP), F[1], ALU.mult, ALU.add))
            step(tt(F[6], F[3], F[4], ALU.add))
            step(ts(F[6], F[6], float(E - 1), None, ALU.add))
            step(tt(F[6], F[6], F[2], ALU.subtract))
            step(ts(F[7], F[4], 1.0, None, ALU.min))
            step(tt(F[6], F[6], F[7], ALU.mult))
            step(tt(F[6], F[6], F[2], ALU.add))
            step(tt(slot1h[0:C], const("iota", C).unsqueeze(1).to_broadcast([C, 2 * NC, 128]), per(F[5], 128), ALU.is_equal))
            step(tt(blk1h[0:C], const("iota", C)[:, 0:BLOCKS].unsqueeze(1).to_broadcast([C, 2 * NC, BLOCKS]),
                    per(F[6], BLOCKS), ALU.is_equal))
            tok = const("tok", C)
            for k in range(2):
                kk = slice(k, 2 * NC, 2)
                step(tt(vals[0:C, kk, 0, :], blk1h[0:C, kk, :], per(tok, BLOCKS), ALU.mult))
            step(tt(vals[0:C, :, 1, :], blk1h[0:C], per(const("dst", C), BLOCKS), ALU.mult))
            n = step(tt(vals[0:C, :, 2, :], blk1h[0:C], per(F[0], BLOCKS), ALU.mult))
            assert n == TABLE_IN, (n, "TABLE_IN")
            dve.wait_ge(r_pe, 2)
            tab = bank[2][:, 0:3 * BLOCKS].rearrange("p (a b) -> p a b", a=3)
            step(ts(ttab.rearrange("p b a -> p a b"), tab[:, 0:2, :], float(BIG), None, ALU.add))
            step(nc.vector.tensor_copy(itab, ttab))
            nc.vector.tensor_copy(wtab, tab[:, 2, :]).then_inc(tables, 1)
            dve.wait_ge(tables, 1)
            if stop == "route":
                return
            for p in range(2):
                nc.vector.memset(xg[p], 0.0).then_inc(xg_zero, 1)

            def columns(eg, pg, es, ps):
                if eg is not None:
                    nc.vector.tensor_copy(gi[pg], itab[:, eg, 0:1] if isinstance(eg, int) else
                                          itab[:, bass.ds(eg, 1), 0:1].rearrange("p o n -> p (o n)"))
                if es is not None:
                    b = slice(es, es + 1) if isinstance(es, int) else bass.ds(es, 1)
                    nc.vector.tensor_copy(si[ps], itab[:, b, 1:2].rearrange("p o n -> p (o n)"))
                    m = nc.vector.tensor_copy(wcol[ps], wtab[:, b])
                    m.then_inc(icol, 1)

            columns(0, 0, None, None)
            nc.vector.tensor_copy(gi[1], itab[:, 1, 0:1]).then_inc(icol, 1)

            def turned(e, p):
                dve.wait_ge(xt_e, e + 1)
                nc.vector.tensor_copy(xgT[p][:, 4:8, :], bank[6][:, :].rearrange("p (k n) -> p k n", k=4)).then_inc(xte_dve, 1)

            def hidden(e, p):
                dve.wait_ge(silu_e, e + 1)
                dve.wait_ge(u_done, e + 1)
                nc.vector.tensor_tensor(hid, bank[2][:, :], gs[p], ALU.mult).then_inc(hid_done, 1)

            def y_out(e, p):
                dve.wait_ge(d_done, e + 1)
                nc.vector.tensor_scalar(ysb[p][:, 512:D], bank[4][:, :], wcol[p], None, ALU.mult).then_inc(y_dve, 1)

            turned(0, 0)
            nc.vector.tensor_copy(gi[0], itab[:, 2, 0:1]).then_inc(gi2_done, 1)
            turned(1, 1)
            columns(3, 1, 0, 0)
            hidden(0, 0)

            def expert(e, p):
                y_out(e - 1, 1 - p)
                turned(e + 1, 1 - p)
                columns(e + 3, 1 - p, e, p)
                hidden(e, p)

            with dve.Fori(0, E // 2 - 1) as j:
                expert(j * 2 + 1, 1)
                expert(j * 2 + 2, 0)
            y_out(E - 2, 0)
            dve.wait_ge(scattered, 16 * (E - 2))
            columns(None, None, E - 1, 1)
            hidden(E - 1, 1)
            y_out(E - 1, 1)

            def over(j):
                dve.wait_ge(scattered, (j + E) * 16)
                columns(j + E, 0, j + E, 0)
                turned(j + E, 0)
                hidden(j + E, 0)
                dve.wait_ge(icol, j + E + 2)
                y_out(j + E, 0)

            over_loop(dve, over)
            dve.wait_ge(fw_loaded, 16)
            with dve.Fori(0, FT // 2) as i:
                for u in range(2):
                    t = i * 2 + u
                    dve.wait_ge(hf_loaded[u], i * 16 + 16)
                    dve.wait_ge(yf_loaded[u], i * 16 + 16)
                    nc.vector.tensor_tensor(hf[u], hf[u], yf[u][:, 0:D], ALU.add).then_inc(f_sum, 1)
                    dve.wait_ge(f_sum, t + 1)
                    nc.vector.tensor_tensor(hf[u], hf[u], yf[u][:, D:2 * D], ALU.add).then_inc(f_add, 1)
                    dve.wait_ge(f_rstd, t + 1)
                    nc.vector.scalar_tensor_tensor(of[u], hf[u], stat[:, u, 2:3], fw, ALU.mult, ALU.mult).then_inc(f_out, 1)

        def tail_pool(pool):
            last_row, last_choice = pool.to_reg(L - 1), pool.to_reg(2 * L - 1)
            pool.wait_ge(oy_done, H)

            def stage(t, u):
                cols = slice(t * C, (t + 1) * C) if isinstance(t, int) else bass.ds(t * C, C)
                nc.gpsimd.tensor_copy(y_st[u], yT[:, :, cols]).then_inc(yst_done, 1)

            stage(0, 0)
            stage(1, 1)
            with pool.Fori(0, NC // 2 - 1) as i:
                for u in range(2):
                    pool.wait_ge(out_done, i * 4 + 2 * u + 2)
                    stage(i * 2 + u + 2, u)
            if stop == "route":
                return

            def gather(p):
                nc.gpsimd.indirect_dma_start(out=xg[p], out_offset=None, in_=xn_dram,
                                             in_offset=bass.IndirectOffsetOnAxis(ap=gi[p], axis=0),
                                             bounds_check=last_row, oob_is_err=False).then_inc(gathered[p], 16)

            def scatter(e, p):
                pool.wait_ge(icol, e + 2)
                pool.wait_ge(y_act, e + 1)
                pool.wait_ge(y_dve, e + 1)
                nc.gpsimd.indirect_dma_start(out=y_dram, out_offset=bass.IndirectOffsetOnAxis(ap=si[p], axis=0),
                                             in_=ysb[p], in_offset=None,
                                             bounds_check=last_choice, oob_is_err=False).then_inc(scattered, 16)
                pool.wait_ge(scattered, (e + 1) * 16)

            pool.wait_ge(xg_zero, 2)
            pool.wait_ge(x2_stored, 16 * NC)
            pool.wait_ge(icol, 1)
            gather(0)
            gather(1)
            pool.wait_ge(gi2_done, 1)
            pool.wait_ge(xte_act, 1)
            gather(0)
            for e in range(E):
                scatter(e, e % 2)
                if e + 3 < E:
                    gather((e + 3) % 2)
            total = pool.value_load(over_i[0:1, OVER:OVER + 1], min_val=0, max_val=OVER)
            for j in range(OVER):
                with pool.If(total > j):
                    pool.wait_ge(icol, j + E + 2)
                    gather(0)
                    scatter(j + E, 0)
            nc.gpsimd.memset(stat[0:1, 0, 3:4], 0.0).then_inc(moe_done, 1)

        block = ctx.enter_context(nc.Block())

        def tile_done(h, kind, pieces=3):
            return h * 21 + 9 + 3 * kind + pieces

        ACT_ORDER = [Z, GC, Q, K, V]

        def by_act(h, kind, pieces=3):
            return h * 15 + 9 + 3 * ACT_ORDER.index(kind) + pieces

        def by_dve(h, kind, pieces=3):
            return h * 6 + 3 * (kind - UU) + pieces

        ROUNDS = ["grow", "vtr", "ktr", "gk", "gq", "mtr", "ttr0"]
        for n in range(1, LEVELS):
            ROUNDS += [f"z{n}", f"rz{n}"] + ([f"ttr{n}"] if n < LEVELS - 1 else [])
        DVE_R = [r for r in ROUNDS if r in ("grow", "vtr", "ktr", "gk", "gq", "mtr") or r.startswith("rz")]
        ACT_R = [r for r in ROUNDS if r == "grow" or r not in DVE_R]

        def at(order, h, name, g):
            return h * (3 * len(order)) + 3 * order.index(name) + g + 1

        SUMS = ["mix", "o", "q", "k"]

        def sums(h, name, pieces=3):
            return h * 12 + 6 + 3 * SUMS.index(name) + pieces

        def chunk(a, c):
            return a[:, c * C:(c + 1) * C]

        def bmat(g, w=C):
            n = len(GROUPS[g])
            return bank[3 + g][:, 0:n * w].rearrange("p (a b) -> p a b", a=n)

        def gsl(g):
            return slice(GROUPS[g].start, GROUPS[g].stop)

        @block.sync
        def _(sp):
            sp.dma_start(const_sb, consts).then_inc(s_const, 16)
            sp.dma_start(par_sb, par).then_inc(s_const, 16)
            for u in range(2):
                sp.dma_start(x_sb[u][0:C, :], x[u * C:(u + 1) * C, :]).then_inc(x_loaded[u], 16)
            for s, kind in ((0, Q), (1, K), (2, V), (3, KINDS + GB)):
                n = s if s < 3 else 3 + GB
                sp.dma_start(wst[s], wt[n].rearrange("p (k n) -> p k n", k=KD)).then_inc(w_loaded[s], 16)
            with sp.Fori(0, NC // 2 - 1) as i:
                for u in range(2):
                    sp.wait_ge(xn_done, i * 2 + u + 1)
                    sp.dma_start(x_sb[u][0:C, :], x[bass.ds((i * 2 + u + 2) * C, C), :]).then_inc(x_loaded[u], 16)

            def load_w(s, n):
                sp.dma_start(wst[s], wt[bass.ds(n, 1)].rearrange("o p (k n) -> (o p) k n", k=KD)
                             if not isinstance(n, int) else wt[n].rearrange("p (k n) -> p k n", k=KD)
                             ).then_inc(w_loaded[s], 16)

            for s in range(3):
                sp.wait_ge(proj_done, 3 * (s + 1))
                load_w(s, 3 + s)
            with sp.Fori(0, H - 1) as h:
                for s in range(3):
                    sp.wait_ge(proj_done, tile_done(h, s))
                    load_w(s, h * 7 + 3 + Q + s)
                sp.wait_ge(proj_done, tile_done(h, GB))
                load_w(3, h * 7 + 10 + GB)
                for s in range(3):
                    sp.wait_ge(proj_done, tile_done(h, Q + s))
                    load_w(s, h * 7 + 10 + s)
            h = H - 1
            sp.wait_ge(proj_done, tile_done(h, GB))
            sp.dma_start(wo_sb, w_out.rearrange("(k p) n -> p k n", p=128)).then_inc(s_wout, 16)
            if stop == "mixer":
                return
            tail_sync(sp)

        def project(pe, kind, pc, slot):
            o, n = PIECE[pc]
            for k in range(KD):
                m = nc.tensor.matmul(bank[pc][:, 0:n], wst[slot][:, k, :], xnT[:, k, o:o + n],
                                     start=(k == 0), stop=(k == KD - 1))
            m.then_inc(proj_done, 1)

        def sum_pieces(pe, h, name, src, mat, first=0):
            base = first + 3 * (SUMS.index(name) if h is not None else 0)
            for pc, (o, n) in enumerate(PIECE):
                b = 6 + (base + pc) % 2
                if h is None:
                    if base + pc >= 2:
                        pe.wait_ge(sum_act, base + pc - 1)
                else:
                    pe.wait_ge(sum_act, sums(h, name, pc - 1))
                nc.tensor.matmul(bank[b][:, 0:n], mat, src[:, o:o + n], start=True, stop=True).then_inc(sum_done, 1)

        @block.tensor
        def _(pe):
            pe.wait_ge(s_const, 32)
            with pe.Fori(0, NC // 2) as i:
                for u in range(2):
                    pe.wait_ge(xn_done, i * 2 + u + 1)
                    for b in range(2):
                        for k in range(4):
                            m = nc.tensor.transpose(bank[2 * u + b][:, k * C:(k + 1) * C],
                                                    xn_sb[u][0:C, (4 * b + k) * 128:(4 * b + k + 1) * 128],
                                                    ident[0:C, 0:C])
                        m.then_inc(xt_done, 1)
            pe.wait_ge(xnT_done, 2 * NC)
            for s in range(3):
                pe.wait_ge(w_loaded[s], 16)
                for pc in range(3):
                    if s:
                        pe.wait_ge(proj_act, 3 * (s - 1) + pc + 1)
                    project(pe, Q + s, pc, s)
            for c in range(NC):
                for k in range(KD):
                    m = nc.tensor.matmul(bank[7][0:C, c * 8:c * 8 + 8], xnT[:, k, c * C:(c + 1) * C], wab[:, k, :],
                                         start=(k == 0), stop=(k == KD - 1))
            m.then_inc(ab_done, 1)
            pe.wait_ge(gt_done, 1)
            gf = g_tok[0:C].rearrange("p h c -> p (h c)")
            nc.tensor.matmul(bank[6][0:C, 0:40], incl, gf, start=True, stop=True)
            nc.tensor.matmul(bank[6][:, 64:104], ones[0:C, :], gf, start=True, stop=True).then_inc(gsum_done, 1)
            pe.wait_ge(gates_dve, 6)
            pe.wait_ge(gates_act, 6)
            for n, s in enumerate(("q", "k")):
                pe.wait_ge(sq_done, n + 1)
                sum_pieces(pe, None, s, sq[n], ones, first=3 * n)

            def fill(h, kind, pc):
                s = kind % 4 if kind < Q else kind - Q
                if pc == 0:
                    pe.wait_ge(w_loaded[s], (h + 1) * 16 if kind == GB else
                               (h * 2 + (2 if kind < GB else 3)) * 16)
                if kind == Z:
                    pe.wait_ge(proj_act, h * 15 + 6 + pc + 1)
                elif kind in (GC, UU):
                    pe.wait_ge(proj_act, by_act(h, kind - 1, pc + 1))
                elif kind in (GB, Q):
                    pe.wait_ge(proj_dve, by_dve(h, kind - 1, pc + 1))
                else:
                    pe.wait_ge(proj_act, by_act(h, kind - 1, pc + 1))
                project(pe, kind, pc, s)

            def rnd(h, name):
                prev = ROUNDS[ROUNDS.index(name) - 1] if name != "grow" else None
                for g in range(3):
                    if prev in ACT_R:
                        pe.wait_ge(gdn_act, at(ACT_R, h, prev, g))
                    if prev in DVE_R:
                        pe.wait_ge(gdn_dve, at(DVE_R, h, prev, g))
                    if name.startswith("z") and g == 0:
                        pe.wait_ge(a_done, h * LEVELS + int(name[1:]) + 1)
                    if name == "ttr0" and g == 0:
                        pe.wait_ge(t0_done, h + 1)
                    if name == "vtr" and g == 0:
                        pe.wait_ge(silu_done, h * 3 + 3)
                    if name == "ktr" and g == 0:
                        pe.wait_ge(qk_done, h * 2 + 2)
                    if name == "grow" and g == 0:
                        pe.wait_ge(head_done, h + 1)
                    if name.startswith("rz") and name != "rz1":
                        pe.wait_ge(gdn_act, at(ACT_R, h, "ttr" + str(int(name[2:]) - 1), g))
                    for n, c in enumerate(GROUPS[g]):
                        o = bmat(g)[0:C, n, :]
                        if name == "grow":
                            m = nc.tensor.matmul(bmat(g)[:, n, :], gbc[0:C, c, :], incl, start=True, stop=True)
                        elif name in ("vtr", "ktr"):
                            m = nc.tensor.transpose(bmat(g, 128)[0:C, n, :], chunk(vT if name == "vtr" else kT, c), ident)
                        elif name in ("gk", "gq"):
                            m = nc.tensor.matmul(o, chunk(kT, c), chunk(kT if name == "gk" else qT, c),
                                                 start=True, stop=True)
                        elif name == "mtr":
                            m = nc.tensor.transpose(o, mT[0:C, c, :], ident[0:C, 0:C])
                        elif name == "ttr0":
                            m = nc.tensor.transpose(o, tI[0:C, c, :], ident[0:C, 0:C])
                        elif name.startswith("ttr"):
                            m = nc.tensor.transpose(o, rT[0:C, c, :], ident[0:C, 0:C])
                        elif name.startswith("rz"):
                            m = nc.tensor.matmul(o, tI[0:C, c, :], zz[0:C, c, :], start=True, stop=True)
                        else:
                            m = nc.tensor.matmul(o, aL[int(name[1:]) % 2][0:C, c, :], rT[0:C, c, :],
                                                 start=True, stop=True)
                    m.then_inc(gdn_done, 1)

            def scan(h, last):
                pe.wait_ge(sum_act, sums(h, "mix"))
                pe.wait_ge(qg_done, h + 1)
                for g in range(3):
                    pe.wait_ge(gdn_dve, at(DVE_R, h, "rz" + str(LEVELS - 1), g))
                for c in range(NC):
                    pe.wait_ge(s_done, h * (NC + 1) + c + 1)
                    nc.tensor.matmul(bank[3][0:C, 0:128], chunk(kT, c), state, start=True, stop=True).then_inc(ks_done, 1)
                    if not last and c < 9:
                        fill(h, Q + c // 3, c % 3)
                    if c:
                        pe.wait_ge(o_done, h * NC + c)
                    nc.tensor.matmul(bank[5][:, 0:C], state, chunk(qg, c), start=True, stop=False)
                    pe.wait_ge(r_done, h * NC + c + 1)
                    nc.tensor.matmul(bank[4][0:C, 0:128], rT[0:C, c, :], r_sb[0:C, :],
                                     start=True, stop=True).then_inc(vnp_done, 1)
                    pe.wait_ge(vn_done, h * NC + c + 1)
                    nc.tensor.matmul(bank[5][:, 0:C], vn_sb[0:C, :], dTi[0:C, c, :], start=False, stop=True)
                    nc.tensor.matmul(bank[6][:, 0:128], kd[0:C, c, :], vn_sb[0:C, :],
                                     start=True, stop=True).then_inc(ods_done, 1)
                pe.wait_ge(s_done, h * (NC + 1) + NC + 1)
                pe.wait_ge(o_done, h * NC + NC)

            def mixer(h, last):
                fill(h, Z, 0)
                fill(h, Z, 1)
                rnd(h, "grow")
                fill(h, Z, 2)
                rnd(h, "vtr")
                rnd(h, "ktr")
                fill(h, GC, 0)
                rnd(h, "gk")
                fill(h, GC, 1)
                rnd(h, "gq")
                rnd(h, "mtr")
                fill(h, GC, 2)
                rnd(h, "ttr0")
                fills = [(UU, 0), (UU, 1), (UU, 2), (GB, 0), (GB, 1), (GB, 2)]
                for n in range(1, LEVELS):
                    rnd(h, f"z{n}")
                    if fills:
                        fill(h, *fills.pop(0))
                    rnd(h, f"rz{n}")
                    if fills:
                        fill(h, *fills.pop(0))
                    if n == 5:
                        pe.wait_ge(sq_done, h * 4 + 3)
                        sum_pieces(pe, h, "mix", sq[0], bones)
                    if n < LEVELS - 1:
                        rnd(h, f"ttr{n}")
                scan(h, last)
                pe.wait_ge(sq_done, h * 4 + (5 if not last else 4))
                sum_pieces(pe, h, "o", sq[1], ones)
                if not last:
                    sum_pieces(pe, h, "q", sq[0], ones)
                    pe.wait_ge(sq_done, h * 4 + 6)
                    sum_pieces(pe, h, "k", sq[1], ones)

            with pe.Fori(0, H - 1) as h:
                mixer(h, False)
            mixer(H - 1, True)
            if stop == "mixer":
                return
            tail_tensor(pe)

        @block.scalar
        def _(act):
            act.wait_ge(s_const, 32)
            with act.Fori(0, NC // 2) as i:
                for u in range(2):
                    act.wait_ge(x_loaded[u], i * 16 + 16)
                    nc.scalar.activation(junk[0:C, :], x_sb[u][0:C, :], ACT.Square,
                                         accum_out=stat[0:C, u, 0:1]).then_inc(ss_done, 1)
                    act.wait_ge(ss_done, i * 4 + 2 * u + 1)
                    nc.scalar.activation(stat[0:C, u, 1:2], stat[0:C, u, 0:1], ACT.Ln, scale=1.0 / D,
                                         bias=eps[0:C, :]).then_inc(ss_done, 1)
                    act.wait_ge(ss_done, i * 4 + 2 * u + 2)
                    nc.scalar.activation(stat[0:C, u, 2:3], stat[0:C, u, 1:2], ACT.Exp, scale=-0.5).then_inc(rstd_done, 1)
            act.wait_ge(zeros_done, 2)

            def evac_raw(pc, buf):
                o, n = PIECE[pc]
                nc.scalar.activation(raw[buf][:, 3 + o:3 + o + n], bank[pc][:, 0:n], ACT.Copy).then_inc(proj_act, 1)

            def silu(dst, n):
                nc.scalar.activation(dst, cv[n], ACT.Silu).then_inc(silu_done, 1)

            def norm(first, count, buf, scale, shift):
                for pc, (o, n) in enumerate(PIECE):
                    act.wait_ge(sum_done, count(pc + 1))
                    nc.scalar.activation(rs[buf][:, o:o + n], bank[6 + (first + pc) % 2][:, 0:n], ACT.Ln,
                                         scale=scale, bias=eps).then_inc(sum_act, 1)
                act.wait_ge(sum_act, count(3))
                kw = {"bias": shift} if shift is not None else {}
                nc.scalar.activation(rs[buf], rs[buf], ACT.Exp, scale=-0.5, **kw).then_inc(rs_done, 1)

            qb = const("qb")
            for s in range(3):
                if s == 2:
                    act.wait_ge(conv_step, 4)
                for pc in range(3):
                    act.wait_ge(proj_done, 3 * s + pc + 1)
                    evac_raw(pc, s % 2)
            for s, dst in enumerate((cv[0], cv[1], vT)):
                act.wait_ge(conv_step, 4 * s + 4)
                silu(dst, s)
            ab = bank[7][0:C, 0:80].rearrange("p (c n) -> p n c", n=8)
            act.wait_ge(gates_dve, 1)
            nc.scalar.activation(small[0:C, 1, :], small[0:C, 1, :], ACT.Exp, scale=-1.0).then_inc(gates_act, 1)
            nc.scalar.activation(ea[0:C, :], param("alog", C), ACT.Exp).then_inc(gates_act, 1)
            nc.scalar.activation(small[0:C, 2, :].rearrange("p (h c) -> p h c", h=H), ab[:, 4:8, :], ACT.Exp,
                                 scale=-1.0).then_inc(gates_act, 1)
            act.wait_ge(gates_act, 3)
            nc.scalar.activation(small[0:C, 1, :], small[0:C, 1, :], ACT.Ln, bias=1.0).then_inc(gates_act, 1)
            act.wait_ge(gates_dve, 6)
            nc.scalar.activation(small[0:C, 3, :], bank[6][0:C, 0:40], ACT.Exp).then_inc(gates_act, 1)
            nc.scalar.activation(a_last.rearrange("p h c -> p (h c)"), bank[6][:, 64:104], ACT.Exp).then_inc(gates_act, 1)
            nc.scalar.activation(tok_sc[0:C, :, 3, :], tok_sc[0:C, :, 3, :], ACT.Exp).then_inc(gates_act, 1)
            norm(0, lambda p: p, 0, 1.0, qb)
            norm(3, lambda p: 3 + p, 1, 1.0, None)

            def grp(h, name, dst, func):
                for g in range(3):
                    act.wait_ge(gdn_done, at(ROUNDS, h, name, g))
                    n = len(GROUPS[g])
                    if name == "grow":
                        act.wait_ge(gdn_dve, at(DVE_R, h, name, g))
                        nc.scalar.activation(eG[:, GROUPS[g].start * C:GROUPS[g].stop * C], bank[3 + g][:, 0:n * C],
                                             func).then_inc(gdn_act, 1)
                    else:
                        nc.scalar.activation(dst[0:C, gsl(g), :], bmat(g)[0:C], func).then_inc(gdn_act, 1)

            def mixer(h, last):
                grp(h, "grow", None, ACT.Exp)
                act.wait_ge(gdn_dve, at(DVE_R, h, "grow", 2))
                nc.scalar.activation(dT[0:C], dT[0:C], ACT.Exp).then_inc(dexp_done, 1)
                for pc, (o, n) in enumerate(PIECE):
                    act.wait_ge(proj_done, tile_done(h, Z, pc + 1))
                    nc.scalar.activation(zs[:, o:o + n], bank[pc][:, 0:n], ACT.Silu).then_inc(proj_act, 1)
                for pc in range(3):
                    act.wait_ge(proj_done, tile_done(h, GC, pc + 1))
                    evac_raw(pc, 0)
                grp(h, "ttr0", rT, ACT.Copy)
                for n in range(1, LEVELS):
                    grp(h, f"z{n}", zz, ACT.Copy)
                    if n == 5:
                        norm(0, lambda p: sums(h, "mix", p), 0, 1.0 / 64, None)
                    if n < LEVELS - 1:
                        grp(h, f"ttr{n}", tI, ACT.Copy)
                for c in range(NC):
                    act.wait_ge(vnp_done, h * NC + c + 1)
                    nc.scalar.activation(vn_sb[0:C, :], bank[4][0:C, 0:128], ACT.Copy).then_inc(vn_done, 1)
                    if not last and c < 9:
                        act.wait_ge(proj_done, tile_done(h, Q + c // 3, c % 3 + 1))
                        if c == 6:
                            act.wait_ge(conv_step, h * 15 + 19)
                        evac_raw(c % 3, (c // 3) % 2)
                    act.wait_ge(ods_done, h * NC + c + 1)
                    nc.scalar.activation(chunk(oT, c), bank[5][:, 0:C], ACT.Copy).then_inc(o_done, 1)
                    if not last and c == 6:
                        act.wait_ge(conv_step, h * 15 + 19)
                        silu(cv[0], 0)
                if not last:
                    act.wait_ge(conv_step, h * 15 + 23)
                    silu(cv[1], 1)
                    act.wait_ge(conv_step, h * 15 + 27)
                    silu(vT, 2)
                norm(1, lambda p: sums(h, "o", p), 1, 1.0 / 128, None)
                if not last:
                    act.wait_ge(mixy_done, h + 1)
                    norm(0, lambda p: sums(h, "q", p), 0, 1.0, qb)
                    act.wait_ge(oy_part, h + 1)
                    norm(1, lambda p: sums(h, "k", p), 1, 1.0, None)

            with act.Fori(0, H - 1) as h:
                mixer(h, False)
            mixer(H - 1, True)
            if stop == "mixer":
                return
            tail_scalar(act)

        @block.vector
        def _(dve):
            for u in range(2):
                nc.vector.memset(raw[u][:, 0:3], 0.0).then_inc(zeros_done, 1)
            dve.wait_ge(s_const, 32)
            mw = mixw.unsqueeze(2).to_broadcast([128, KD, C])
            with dve.Fori(0, NC // 2) as i:
                for u in range(2):
                    dve.wait_ge(rstd_done, i * 2 + u + 1)
                    nc.vector.tensor_scalar(xn_sb[u][0:C, :], x_sb[u][0:C, :], stat[0:C, u, 2:3], None,
                                            ALU.mult).then_inc(xn_done, 1)
                    for b in range(2):
                        dve.wait_ge(xt_done, i * 4 + 2 * u + b + 1)
                        nc.vector.tensor_tensor(xnT[:, 4 * b:4 * b + 4, bass.ds((i * 2 + u) * C, C)],
                                                bank[2 * u + b][:, 0:4 * C].rearrange("p (k c) -> p k c", k=4),
                                                mw[:, 4 * b:4 * b + 4, :], ALU.mult).then_inc(xnT_done, 1)

            def conv(n, buf, taps_n, ntap, base):
                dst = cv[n]
                for j in range(ntap):
                    src = raw[buf][:, 4 - ntap + j:4 - ntap + j + L]
                    t = taps[:, taps_n + j:taps_n + j + 1]
                    if j:
                        dve.wait_ge(conv_step, base + j)
                        m = nc.vector.scalar_tensor_tensor(dst, src, t, dst, ALU.mult, ALU.add)
                    else:
                        m = nc.vector.tensor_scalar(dst, src, t, None, ALU.mult)
                    m.then_inc(conv_step, 1)
                    yield

            nc.vector.tensor_copy(taps, taps_all[:, 0:16]).then_inc(taps_done, 1)
            dve.wait_ge(taps_done, 1)
            for s in range(3):
                dve.wait_ge(proj_act, 3 * s + 3)
                for _ in conv(s, s % 2, 4 * s, 4, 4 * s):
                    pass

            ab = bank[7][0:C, 0:80].rearrange("p (c n) -> p n c", n=8)
            t = [small[0:C, n, :].rearrange("p (h c) -> p h c", h=H) for n in range(4)]
            dve.wait_ge(ab_done, 1)
            nc.vector.tensor_tensor(t[0], ab[:, 0:4, :], param("dt", C).unsqueeze(2).to_broadcast([C, H, NC]),
                                    ALU.add).then_inc(adt_done, 1)
            dve.wait_ge(adt_done, 1)
            nc.vector.scalar_tensor_tensor(t[1], t[0], -1.0, t[0], ALU.mult, ALU.max).then_inc(gates_dve, 1)
            dve.wait_ge(gates_act, 4)
            nc.vector.scalar_tensor_tensor(t[0], t[0], 0.0, t[1], ALU.max, ALU.add).then_inc(gates_dve, 1)
            nc.vector.tensor_scalar(t[2], t[2], 1.0, None, ALU.add).then_inc(gates_dve, 1)
            dve.wait_ge(gates_dve, 3)
            nc.vector.scalar_tensor_tensor(g_tok[0:C], t[0], -1.0, ea[0:C].unsqueeze(2).to_broadcast([C, H, NC]),
                                           ALU.mult, ALU.mult).then_inc(gt_done, 1)
            nc.vector.reciprocal(tok_sc[0:C, :, 1, :], t[2]).then_inc(gates_dve, 1)
            dve.wait_ge(gsum_done, 1)
            gc_ps = bank[6][0:C, 0:40].rearrange("p (h c) -> p h c", h=H)
            gl_ps = bank[6][0:C, 64:104].rearrange("p (h c) -> p h c", h=H)
            nc.vector.tensor_copy(tok_sc[0:C, :, 0, :], gc_ps).then_inc(gates_dve, 1)
            dve.wait_ge(gates_dve, 5)
            nc.vector.tensor_tensor(tok_sc[0:C, :, 3, :], gl_ps, tok_sc[0:C, :, 0, :], ALU.subtract).then_inc(gates_dve, 1)
            dve.wait_ge(gates_act, 5)
            nc.vector.scalar_tensor_tensor(tok_sc[0:C, :, 2, :], tok_sc[0:C, :, 1, :], -1.0, t[3], ALU.mult,
                                           ALU.mult).then_inc(gates_dve, 1)

            def head_copies(h):
                dve.wait_ge(gates_dve, 7)
                dve.wait_ge(gates_act, 7)
                hh = slice(h, h + 1) if isinstance(h, int) else bass.ds(h, 1)
                nc.vector.tensor_copy(head_sc[0:C].rearrange("p (o k) c -> p o k c", o=1), tok_sc[0:C, hh])
                nc.vector.tensor_copy(head_a.rearrange("p (o c) -> p o c", o=1), a_last[:, hh])
                nc.vector.tensor_copy(gbc[0:C].rearrange("p (o c) n -> p (o c) n", o=1),
                                      g_tok[0:C, hh].rearrange("p o c -> p (o c)").unsqueeze(2).to_broadcast([C, NC, 128])
                                      ).then_inc(head_done, 1)

            def q_or_k(n, count):
                dve.wait_ge(rs_done, count)
                nc.vector.tensor_tensor((qT, kT)[n], cv[n], rs[n], ALU.mult).then_inc(qk_done, 1)

            head_copies(0)
            q_or_k(0, 1)
            q_or_k(1, 2)

            def grp(h, name):
                for g in range(3):
                    dve.wait_ge(gdn_done, at(ROUNDS, h, name, g))
                    s, n = gsl(g), len(GROUPS[g])

                    def per_token(kind, w):
                        return head_sc[0:C, kind, s].unsqueeze(2).to_broadcast([C, n, w])

                    if name == "grow":
                        nc.vector.tensor_tensor(dT[0:C, s], bmat(g)[0:C], per_token(0, C), ALU.subtract).then_inc(dt_sub, 1)
                        dve.wait_ge(dt_sub, h * 3 + g + 1)
                        m = nc.vector.tensor_scalar(dT[0:C, s], dT[0:C, s], 0.0, None, ALU.min)
                    elif name == "vtr":
                        m = nc.vector.tensor_tensor(bv[0:C, s], bmat(g, 128)[0:C], per_token(1, 128), ALU.mult)
                    elif name == "ktr":
                        m = nc.vector.tensor_tensor(kd[0:C, s], bmat(g, 128)[0:C], per_token(3, 128), ALU.mult)
                    elif name == "gk":
                        m = nc.vector.tensor_tensor(mT[0:C, s], bmat(g)[0:C], dTs[0:C, s], ALU.mult)
                    elif name == "gq":
                        m = nc.vector.tensor_tensor(dTi[0:C, s], bmat(g)[0:C], dTi[0:C, s], ALU.mult)
                    elif name == "mtr":
                        m = nc.vector.tensor_tensor(lM[0:C, s], bmat(g)[0:C], per_token(1, C), ALU.mult)
                    else:
                        m = nc.vector.tensor_tensor(rT[0:C, s], rT[0:C, s], bmat(g)[0:C], ALU.subtract)
                    m.then_inc(gdn_dve, 1)

            def mixer(h, last):
                nc.vector.memset(state, 0.0).then_inc(s_done, 1)
                hn = slice((h + 1) * 16, (h + 2) * 16) if isinstance(h, int) else bass.ds((h + 1) * 16, 16)
                nc.vector.tensor_copy(taps, taps_all[:, hn]).then_inc(taps_done, 1)
                dve.wait_ge(head_done, h + 1)
                grp(h, "grow")
                dve.wait_ge(dexp_done, h + 1)
                nc.vector.tensor_tensor(dTi[0:C], dT[0:C], incl.unsqueeze(1).to_broadcast([C, NC, C]),
                                        ALU.mult).then_inc(dti_done, 1)
                grp(h, "vtr")
                grp(h, "ktr")
                dve.wait_ge(dts_done, h + 1)
                grp(h, "gk")
                dve.wait_ge(dti_done, h + 1)
                grp(h, "gq")
                grp(h, "mtr")

                def u_piece(pc):
                    o, n = PIECE[pc]
                    dve.wait_ge(proj_done, tile_done(h, UU, pc + 1))
                    dve.wait_ge(proj_act, by_act(h, GC, pc + 1))
                    nc.vector.tensor_tensor(raw[1][:, 3 + o:3 + o + n], bank[pc][:, 0:n], raw[0][:, 3 + o:3 + o + n],
                                            ALU.mult).then_inc(proj_dve, 1)

                def gb_piece(pc):
                    o, n = PIECE[pc]
                    dve.wait_ge(proj_done, tile_done(h, GB, pc + 1))
                    nc.vector.tensor_tensor(cv[0][:, o:o + n], bank[pc][:, 0:n], cv[0][:, o:o + n],
                                            ALU.mult).then_inc(proj_dve, 1)

                u_piece(0)
                grp(h, "rz1")
                u_piece(1)
                u_piece(2)
                grp(h, "rz2")
                dve.wait_ge(proj_dve, by_dve(h, UU))
                dve.wait_ge(taps_done, h + 2)
                for _ in conv(0, 1, 12, 3, h * 15 + 12):
                    pass
                dve.wait_ge(conv_step, h * 15 + 15)
                gb_piece(0)
                gb_piece(1)
                grp(h, "rz3")
                gb_piece(2)
                grp(h, "rz4")
                grp(h, "rz5")
                dve.wait_ge(rs_done, h * 4 + 3)
                yh = slice(h, h + 1) if isinstance(h, int) else bass.ds(h, 1)
                nc.vector.scalar_tensor_tensor(yT[:, yh].rearrange("p o l -> p (o l)"), cv[0], taps[:, 15:16], rs[0],
                                               ALU.mult, ALU.mult).then_inc(mixy_done, 1)
                grp(h, "rz6")

                todo = []
                if not last:
                    base = h * 15 + 15
                    todo = [conv(0, 0, 0, 4, base), conv(1, 1, 4, 4, base + 4)]
                for c in range(NC):
                    dve.wait_ge(ks_done, h * NC + c + 1)
                    nc.vector.scalar_tensor_tensor(r_sb[0:C, :], bank[3][0:C, 0:128], head_sc[0:C, 2, c:c + 1],
                                                   bv[0:C, c, :], ALU.mult, ALU.add).then_inc(r_done, 1)
                    dve.wait_ge(ods_done, h * NC + c + 1)
                    nc.vector.scalar_tensor_tensor(state, state, head_a[:, c:c + 1], bank[6][:, 0:128], ALU.mult,
                                                   ALU.add).then_inc(s_done, 1)
                    if not last and c in (3, 4, 6, 7):
                        if c in (3, 6):
                            dve.wait_ge(proj_act, by_act(h, Q if c == 3 else K))
                        for _ in range(2):
                            next(todo[c // 6])
                if not last:
                    dve.wait_ge(s_done, h * (NC + 1) + NC + 1)
                    head_copies(h + 1)
                    dve.wait_ge(proj_act, by_act(h, V))
                    for _ in conv(2, 0, 8, 4, h * 15 + 23):
                        pass
                dve.wait_ge(rs_done, h * 4 + 4)
                yo = slice(H + h, H + h + 1) if isinstance(h, int) else bass.ds(h + H, 1)
                nc.vector.scalar_tensor_tensor(oT, oT, gw, rs[1], ALU.mult, ALU.mult).then_inc(oy_part, 1)
                dve.wait_ge(oy_part, h + 1)
                nc.vector.tensor_tensor(yT[:, yo].rearrange("p o l -> p (o l)"), oT, zs, ALU.mult).then_inc(oy_done, 1)
                if not last:
                    q_or_k(0, h * 4 + 5)
                    q_or_k(1, h * 4 + 6)

            with dve.Fori(0, H - 1) as h:
                mixer(h, False)
            mixer(H - 1, True)
            if stop == "mixer":
                return
            tail_vector(dve)

        @block.gpsimd
        def _(pool):
            pool.wait_ge(s_const, 32)
            for n in range(2):
                pool.wait_ge(silu_done, n + 1)
                nc.gpsimd.tensor_tensor(sq[n], cv[n], cv[n], ALU.mult).then_inc(sq_done, 1)

            def mixer(h, last):
                for g in range(3):
                    pool.wait_ge(gdn_act, at(ACT_R, h, "grow", g))
                pool.wait_ge(qk_done, h * 2 + 1)
                nc.gpsimd.tensor_tensor(qg, qT, eG, ALU.mult).then_inc(qg_done, 1)
                pool.wait_ge(dexp_done, h + 1)
                nc.gpsimd.tensor_tensor(dTs[0:C], dT[0:C], strict.unsqueeze(1).to_broadcast([C, NC, C]),
                                        ALU.mult).then_inc(dts_done, 1)
                for g in range(3):
                    pool.wait_ge(gdn_dve, at(DVE_R, h, "mtr", g))

                def level(n):
                    nc.gpsimd.tensor_tensor(aL[n % 2][0:C], lM[0:C], lev[:, n, :].unsqueeze(1).to_broadcast([C, NC, C]),
                                            ALU.mult).then_inc(a_done, 1)

                level(0)
                pool.wait_ge(a_done, h * LEVELS + 1)
                pool.wait_ge(dti_done, h + 1)
                pool.wait_ge(dts_done, h + 1)
                nc.gpsimd.tensor_tensor(tI[0:C], ident[0:C, 0:C].unsqueeze(1).to_broadcast([C, NC, C]), aL[0][0:C],
                                        ALU.subtract).then_inc(t0_done, 1)
                for n in range(1, LEVELS):
                    if n == 2:
                        pool.wait_ge(t0_done, h + 1)
                    if n >= 3:
                        pool.wait_ge(gdn_done, at(ROUNDS, h, f"z{n - 2}", 2))
                    if n == 6:
                        pool.wait_ge(proj_dve, by_dve(h, GB))
                        nc.gpsimd.tensor_tensor(sq[0], cv[0], cv[0], ALU.mult).then_inc(sq_done, 1)
                    level(n)
                if not last:
                    pool.wait_ge(sum_done, sums(h, "mix"))
                    pool.wait_ge(silu_done, h * 3 + 4)
                    nc.gpsimd.tensor_tensor(sq[0], cv[0], cv[0], ALU.mult).then_inc(sq_done, 1)
                pool.wait_ge(o_done, h * NC + NC)
                nc.gpsimd.tensor_tensor(sq[1], oT, oT, ALU.mult).then_inc(sq_done, 1)
                if not last:
                    pool.wait_ge(sum_done, sums(h, "o"))
                    pool.wait_ge(silu_done, h * 3 + 5)
                    nc.gpsimd.tensor_tensor(sq[1], cv[1], cv[1], ALU.mult).then_inc(sq_done, 1)

            with pool.Fori(0, H - 1) as h:
                mixer(h, False)
            mixer(H - 1, True)
            if stop == "mixer":
                return
            tail_pool(pool)


def kernel(**inputs):
    import concourse.bacc as bacc
    from concourse.bass_utils import run_bass_kernel_spmd

    a = {k: np.asarray(v) for k, v in inputs.items()}
    w_in = a["w_in"][0]
    cols = [3 * 512 + 3 * 512, 512, 1024, 0, 1536, 2048, 2560]
    order = [(0, Q), (0, K), (0, V)] + [(h + (kind >= Q), kind) for h in range(H) for kind in range(KINDS)]
    wt = np.stack([w_in[:, cols[kind] + 128 * h:cols[kind] + 128 * (h + 1)].reshape(KD, 128, 128).transpose(1, 0, 2)
                   .reshape(128, KD * 128) for h, kind in order[:28]])
    par = np.zeros((128, NPAR), np.float32)

    def put(name, v):
        o, w = PAR[name]
        par[:, o:o + w] = v

    taps = np.zeros((128, 5, 16), np.float32)
    qkv = a["qkv_conv_w"][0].reshape(4, 3, H, 128)
    mix = a["conv_mix_w"][0].reshape(3, H, 128)
    for h in range(H):
        taps[:, h, 0:12] = qkv[:, :, h, :].transpose(2, 1, 0).reshape(128, 12)
        taps[:, h + 1, 12:15] = mix[:, h, :].T
        taps[:, h + 1, 15] = a["conv_mix_norm_w"][0, h * 128:(h + 1) * 128]
    put("taps", taps.reshape(128, 80))
    put("mixw", a["mix_norm_w"][0].reshape(KD, 128).T)
    put("gw", a["gdn_norm_w"][0][:, None])
    put("wab", w_in[:, 3584:3592].reshape(KD, 128, 8).transpose(1, 0, 2).reshape(128, 64))
    wr = np.concatenate([a["w_group"][0], a["w_router"][0].reshape(D, E)], 1)
    put("wr", wr.reshape(KD, 128, 36).transpose(1, 0, 2).reshape(128, KD * 36))
    put("bias", np.concatenate([a["b_group"][0], a["b_router"][0].reshape(E)])[None, :])
    put("alog", a["a_log"][0][None, :])
    put("dt", a["dt_bias"][0][None, :])
    ins = {
        "tokens": np.concatenate([a["meta_tokens"], a["x"][0]], 0),
        "consts": constants(), "par": par, "w_tiles": wt, "w_out": a["w_out"][0],
        "ffn_w": np.broadcast_to(a["ffn_norm_w"][0][None, :], (128, D)),
        "fin_w": np.broadcast_to(a["final_norm_w"][None, :], (128, D)),
        "w_gate": a["w_gate"][0], "w_up": a["w_up"][0], "w_down": a["w_down"][0],
    }
    nc = bacc.Bacc("TRN2", target_bir_lowering=False, num_devices=1)
    arrays, aps = {}, []
    for name, v in ins.items():
        v = np.ascontiguousarray(v)
        arrays["in_" + name] = v
        aps.append(nc.dram_tensor("in_" + name, v.shape, F32, kind="ExternalInput").ap())
    out = nc.dram_tensor("out_y", (L - META, D), F32, kind="ExternalOutput").ap()
    layer_kernel(nc, *aps, out, stop=STOP)
    r = run_bass_kernel_spmd(nc, [arrays], core_ids=[0])
    return r.results[0]["out_y"].reshape(1, L - META, D)
```

```python
from contextlib import ExitStack

import numpy as np

import concourse.bass as bass
from concourse import mybir

F32 = mybir.dt.float32
I32 = mybir.dt.int32
F32R = mybir.dt.float32r
ALU = mybir.AluOpType
ACT = mybir.ActivationFunctionType
AX_X = mybir.AxisListType.X

D = 1024
META = 16
L = META + 1024
KD = D // 128
C = 104
NC = L // C
NB = NC // 2
H = 4
KINDS = 7
Z, GC, UU, GB, Q, K, V = range(KINDS)
PIECE = [(0, 347), (347, 347), (694, 346)]
LEVELS = 7
GROUPS = [range(0, 4), range(4, 8), range(8, 10)]
E = 32
NG = 4
EPG = E // NG
CAP = 128
OVER = (2 * L - 1) // CAP
BLOCKS = E + OVER
MAXQ = -(-L // CAP) - 1
BIG = 4096
FE = 512
GRP_DIFF, TOP_DIFF, RANK_IN, TABLE_IN = 6, 27, 51, 101
EPS = 1e-6
STOP = None
WU = 4096
NCOL = 28 * 1024

CONST = {}
_at = 0
for _n, _w in [("ident", 128), ("ones", 128), ("bones", 128), ("incl", C), ("strict", C), ("lev", LEVELS * C),
               ("iota", 128), ("tok", NC), ("dst", 2 * NC), ("r4", NG), ("r8", EPG), ("eps", 1), ("qb", 1)]:
    CONST[_n] = (_at, _w)
    _at += _w
NCONST = _at
PAR = {}
_at = 0
for _n, _w in [("taps", 5 * 16), ("mixw", KD), ("gw", 1), ("wab", KD * 8), ("wr", KD * 36), ("bias", 36),
               ("alog", H), ("dt", H)]:
    PAR[_n] = (_at, _w)
    _at += _w
NPAR = _at


def constants():
    a = np.zeros((128, NCONST), np.float32)

    def put(name, v):
        o, w = CONST[name]
        a[: v.shape[0], o:o + w] = v

    i = np.arange(128)
    c = np.arange(C)
    put("ident", np.eye(128))
    put("ones", np.ones((128, 128)))
    put("bones", (i[:, None] // 64 == i[None, :] // 64) * 1.0)
    put("incl", (c[None, :] >= c[:, None]) * 1.0)
    put("strict", (c[None, :] > c[:, None]) * 1.0)
    lev = []
    for n in range(LEVELS):
        s = 1 << n
        r, q = c[:, None], c[None, :]
        lev.append((r // (2 * s) == q // (2 * s)) & ((r // s) % 2 == 1) & ((q // s) % 2 == 0))
    put("lev", np.concatenate(lev, 1) * 1.0)
    put("iota", np.broadcast_to(i[None, :], (128, 128)))
    tok = i[:C, None] + C * np.arange(NC)[None, :]
    put("tok", tok - BIG)
    put("dst", (2 * tok[:, :, None] + np.arange(2)[None, None, :] - BIG).reshape(C, 2 * NC))
    put("r4", np.broadcast_to(8 - np.arange(NG)[None, :], (128, NG)))
    put("r8", np.broadcast_to(16 - np.arange(EPG)[None, :], (128, EPG)))
    put("eps", np.full((128, 1), EPS))
    put("qb", np.full((128, 1), -0.5 * np.log(128.0)))
    return a


def layer_kernel(nc, x, consts, par, wt, w_out, ffn_w, fin_w, w_gate, w_up, w_down, out, stop=None):
    ctx = ExitStack()
    with ctx:
        NF = 52952
        arena = ctx.enter_context(nc.sbuf_tensor("arena", [128, NF], F32))
        bank = [ctx.enter_context(nc.psum_tensor(f"bank{i}", [128, 512], F32)) for i in range(8)]
        h_dram = nc.dram_tensor("h_rows", (L, D), F32, kind="Internal").ap()
        xn_dram = nc.dram_tensor("xn_rows", (L, D), F32, kind="Internal").ap()
        y_dram = nc.dram_tensor("y_rows", (2 * L, D), F32, kind="Internal").ap()

        arena_base = nc.sbuf_base - 4 * NF

        def place(name, at, *dims, dtype=F32R):
            n = int(np.prod(dims))
            a = nc.alloc_sbuf_tensor_at(name, [128, n], dtype, offset=arena_base + 4 * at)[:, :]
            return a.rearrange("p (a b) -> p a b", a=dims[0]) if len(dims) == 2 else a

        def sem(name):
            return ctx.enter_context(nc.semaphore(name))

        class Zone:
            def __init__(self, at, end):
                self.at, self.end = at, end

            def take(self, *dims):
                n = int(np.prod(dims))
                a = arena[:, self.at:self.at + n]
                self.at += n
                assert self.at <= self.end, (self.at, self.end)
                if len(dims) == 2:
                    a = a.rearrange("p (a b) -> p a b", a=dims[0])
                if len(dims) == 3:
                    a = a.rearrange("p (a b c) -> p a b c", a=dims[0], b=dims[1])
                return a

        keep = Zone(0, 3544)
        zy = Zone(3544, 3544 + 8320)
        zx = Zone(zy.end, zy.end + 8320)
        GBASE = zx.end
        zg = Zone(GBASE, NF)

        const_sb = keep.take(NCONST)
        par_sb = keep.take(NPAR)

        def const(name, rows=128):
            o, w = CONST[name]
            return const_sb[0:rows, o:o + w]

        def param(name, rows=128):
            o, w = PAR[name]
            return par_sb[0:rows, o:o + w]

        ident, ones, bones = const("ident"), const("ones"), const("bones")
        incl, strict = const("incl", C), const("strict", C)
        lev = const("lev", C).rearrange("p (l j) -> p l j", l=LEVELS)
        eps = const("eps")
        taps_all = param("taps")
        mixw, gw = param("mixw"), param("gw")
        wab = param("wab").rearrange("p (k n) -> p k n", k=KD)
        wr = param("wr").rearrange("p (k n) -> p k n", k=KD)
        tok_sc = keep.take(H, 4, NC)
        a_last = keep.take(H, NC)
        g_tok = keep.take(H, NC)
        head_sc = keep.take(4, NC)
        head_a = keep.take(NC)
        taps = keep.take(16)
        state = keep.take(128)
        small = keep.take(4, 40)
        stat = keep.take(2, 4)
        ea = keep.take(H)
        logits = keep.take(NC, 36)
        itab = keep.take(BLOCKS, 2).bitcast(I32)
        wtab = keep.take(BLOCKS)
        over_i = keep.take(OVER + 1).bitcast(I32)

        yT = zy.take(2 * H, L)
        xnT = zx.take(KD, L)
        raw = [zg.take(1044), zg.take(1044)]
        cv = [zg.take(L) for _ in range(3)]
        sq = [zg.take(L), zg.take(L)]
        rs = [zg.take(L), zg.take(L)]
        qT, kT, vT = zg.take(L), zg.take(L), zg.take(L)
        zs = zg.take(L)
        oT = zg.take(L)
        eG = zg.take(L)
        qg = zg.take(L)
        wst = [zg.take(KD, 128) for _ in range(4)]
        r_sb, vn_sb = zg.take(128), zg.take(128)
        x_at = zg.at
        gbc = zg.take(NC, 128)
        bv = zg.take(NC, 128)
        kd = zg.take(NC, 128)
        dT = zg.take(NC, C)
        dTi = zg.take(NC, C)
        dTs = zg.take(NC, C)
        mT = zg.take(NC, C)
        aL = [zg.take(NC, C), zg.take(NC, C)]
        rT = zg.take(NC, C)
        tI = dT
        zz = dTs
        lM = mT
        zn = Zone(x_at, NF)
        x_sb = [zn.take(D) for _ in range(NC)]
        zn = Zone(zy.end - 8320, zy.end)
        xn_sb = [zn.take(D) for _ in range(NB)]
        junk = zn.take(D)
        nstat = zn.take(3, NC)

        wraw = [place(f"w_raw{m}", o, WU, dtype=F32) for m, o in enumerate((GBASE, GBASE + WU, zy.end - 8320))]
        PAIRS = GBASE + 2 * WU
        w_hi = [place(f"w_hi{m}", PAIRS + 2 * m * WU, WU) for m in range(3)]
        w_lo = [place(f"w_lo{m}", PAIRS + (2 * m + 1) * WU, WU) for m in range(3)]
        zo = Zone(GBASE + 2 * WU, NF)
        h_sb = [zo.take(D), zo.take(D)]
        x2_sb = [zo.take(D), zo.take(D)]
        y_hi = [place(f"y_hi{u}", zo.at + 2 * u * KD * C, KD, C) for u in range(2)]
        y_lo = [place(f"y_lo{u}", zo.at + (2 * u + 1) * KD * C, KD, C) for u in range(2)]
        zo.at += 4 * KD * C
        w_out_hi = place("w_out_hi", zo.at, KD, D)
        zo.at += KD * D
        x2T = zo.take(KD, C)
        ffw = zo.take(D)
        w_out_raw = place("w_out_raw", zy.end, KD, D, dtype=F32)
        w_out_lo = place("w_out_lo", zy.end, KD, D)

        s_const, s_wout, s_ffw = sem("const_loaded"), sem("w_out_loaded"), sem("ffw_loaded")
        x_loaded = [sem(f"x_loaded{s}") for s in range(NB)]
        ss_done, rstd_done = sem("ss_done"), sem("rstd_done")
        xn_done, xt_done, xnT_done = sem("xn_done"), sem("xt_done"), sem("xnT_done")
        zeros_done = sem("zeros_done")
        ab_done, gt_done, gates_dve, gates_act, gsum_done = (sem("ab_done"), sem("g_tok_done"), sem("gates_dve"),
                                                             sem("gates_act"), sem("gsum_done"))
        w_loaded = [sem(f"w_loaded{i}") for i in range(4)]
        proj_done, proj_act, proj_dve = sem("proj_done"), sem("proj_act"), sem("proj_dve")
        head_done = sem("head_done")
        gdn_done, gdn_act, gdn_dve = sem("gdn_done"), sem("gdn_act"), sem("gdn_dve")
        dt_sub, dexp_done = sem("dt_sub"), sem("dexp_done")
        dti_done, dts_done, qg_done = sem("dti_done"), sem("dts_done"), sem("qg_done")
        a_done, t0_done = sem("a_done"), sem("t0_done")
        mixy_done, silu_done, sq_done = sem("mixy_done"), sem("silu_done"), sem("sq_done")
        taps_done, adt_done = sem("taps_done"), sem("adt_done")
        conv_step = sem("conv_step")
        sum_done, sum_act, rs_done = sem("sum_done"), sem("sum_act"), sem("rs_done")
        qk_done, oy_part, oy_done = sem("qk_done"), sem("oy_part"), sem("oy_done")
        s_done, ks_done, r_done = sem("state_done"), sem("ks_done"), sem("r_done")
        vnp_done, vn_done, ods_done, o_done = sem("vnp_done"), sem("vn_done"), sem("ods_done"), sem("o_done")

        wo_hi_done, wo_lo_done, y_hi_done = sem("wo_hi_done"), sem("wo_lo_done"), sem("y_hi_done")
        yst_done, out_done, res_done, x2_done = sem("yst_done"), sem("out_done"), sem("res_done"), sem("x2_done")
        xr_loaded = [sem("xr_loaded0"), sem("xr_loaded1")]
        h_stored, x2_stored = sem("h_stored"), sem("x2_stored")
        ff_stat, ffr_done, tr_done, x2T_done = sem("ff_stat"), sem("ffr_done"), sem("tr_done"), sem("x2T_done")
        lg_ps, lg_done = sem("logits_in_psum"), sem("logits_done")
        w_sem = [sem(f"expert_w_loaded{i}") for i in range(3)]
        hi_done = [sem(f"w_hi_done{i}") for i in range(3)]
        lo_done = [sem(f"w_lo_done{i}") for i in range(3)]

        zr = Zone(zy.end - 8320, zy.end)
        slot1h = zr.take(2 * NC, 128)
        blk1h = zr.take(2 * NC, BLOCKS)
        e1h = [zr.take(NC, E), zr.take(NC, E)]
        ecnt, epre = zr.take(NC, E), zr.take(NC, E)
        e3 = zr.take(NC, E)
        nover, oend, obase, tcnt = zr.take(E), zr.take(E), zr.take(E), zr.take(E)
        grp_v = [zr.take(NC, NG) for _ in range(3)]
        exp_v = [zr.take(NC, EPG) for _ in range(6)]
        tk = [zr.take(NC) for _ in range(8)]
        tk2 = [zr.take(2 * NC) for _ in range(8)]
        ocmp = zr.take(OVER, E)
        ofl = zr.take(OVER + 1)
        ttab = zr.take(BLOCKS, 2)
        zv = Zone(NF - 3 * 2 * NC * BLOCKS, NF)
        vals = zv.take(2 * NC, 3, BLOCKS)

        ze = Zone(zy.end - 8320 + WU, zx.end - D)
        fw = arena[:, zx.end - D:zx.end]
        gs = [ze.take(FE), ze.take(FE)]
        hid = ze.take(FE)
        ysb = [ze.take(D), ze.take(D)]

        def pair(name, *dims):
            n = int(np.prod(dims))
            ze.at += 2 * n
            assert ze.at <= ze.end
            return (place(name + "_hi", ze.at - 2 * n, *dims), place(name + "_lo", ze.at - n, *dims))

        xgT = [pair(f"xgT{p}", KD, 128) for p in range(2)]
        hidT = pair("hidT", 4, 128)
        xg = [ze.take(D), ze.take(D)]
        gi = [ze.take(1).bitcast(I32) for _ in range(2)]
        si = [ze.take(1).bitcast(I32) for _ in range(2)]
        wcol = [ze.take(1) for _ in range(2)]

        r_dve, r_act, r_pe, tables = sem("route_dve"), sem("route_act"), sem("route_pe"), sem("tables_done")
        xg_zero, icol, gathered, scattered = sem("xg_zero"), sem("icol_done"), [sem("gathered0"), sem("gathered1")], [sem("scattered0"), sem("scattered1")]
        xt_e, xte_act, xte_dve = sem("xt_experts"), sem("xte_act"), sem("xte_dve")
        g_done, u_done, silu_e, hid_done = sem("gate_done"), sem("up_done"), sem("silu_e"), sem("hid_done")
        ht_e, hta_done, hte_done, d_done, y_act = (sem("ht_experts"), sem("hta_done"), sem("hte_done"), sem("down_done"),
                                                     sem("y_act"))
        moe_done, gi2_done = sem("moe_done"), sem("gi2_done")
        fw_loaded = sem("fw_loaded")
        f_sum, f_add, f_stat, f_rstd, f_out = sem("f_sum"), sem("f_add"), sem("f_stat"), sem("f_rstd"), sem("f_out")
        f_stored = sem("f_stored")

        FT = (L - META) // 128
        hf_loaded, yf_loaded = [[sem(f"{n}_loaded{t}") for t in range(FT)] for n in ("hf", "yf")]
        zf = Zone(GBASE, NF)
        hf = [zf.take(D) for _ in range(FT)]
        yf = [zf.take(2 * D) for _ in range(FT)]
        of = [zf.take(D) for _ in range(FT)]

        UNIT_SRC = [w_gate, w_up, w_down]

        def load_unit(eng, e, slot):
            src = UNIT_SRC[slot]
            kk = KD if slot < 2 else FE // 128
            if isinstance(e, int):
                s = src[e].rearrange("(k p) n -> p k n", p=128)
            else:
                s = src[bass.ds(e, 1)].rearrange("o (k p) n -> (o p) k n", p=128)
            eng.dma_start(wraw[slot].rearrange("p (k n) -> p k n", k=kk), s).then_inc(w_sem[slot], 16)

        def over_loop(eng, body):
            total = eng.value_load(over_i[0:1, OVER:OVER + 1], min_val=0, max_val=OVER)
            with eng.Fori(0, OVER) as j:
                with eng.If(j < total):
                    body(j)

        def tail_sync(sp):
            sp.wait_ge(oy_done, H)
            sp.dma_start(ffw, ffn_w).then_inc(s_ffw, 16)
            for u in range(2):
                sp.dma_start(h_sb[u][0:C, :], x[u * C:(u + 1) * C, :]).then_inc(xr_loaded[u], 16)

            def store(i, u, t):
                rows = slice(t * C, (t + 1) * C) if isinstance(t, int) else bass.ds(t * C, C)
                sp.wait_ge(res_done, (t + 1) * 2)
                sp.dma_start(h_dram[rows, :], h_sb[u][0:C, :]).then_inc(h_stored, 16)
                sp.wait_ge(x2_done, t + 1)
                sp.dma_start(xn_dram[rows, :], x2_sb[u][0:C, :]).then_inc(x2_stored, 16)
                sp.wait_ge(h_stored, (t + 1) * 16)
                sp.wait_ge(x2_stored, (t + 1) * 16)

            with sp.Fori(0, NC // 2 - 1) as i:
                for u in range(2):
                    store(i, u, i * 2 + u)
                    sp.dma_start(h_sb[u][0:C, :], x[bass.ds((i * 2 + u + 2) * C, C), :]).then_inc(xr_loaded[u], 16)
            for u in range(2):
                store(None, u, NC - 2 + u)
            sp.wait_ge(tables, 1)
            load_unit(sp, 0, 2)
            sp.dma_start(fw, fin_w).then_inc(fw_loaded, 16)
            if stop == "route":
                sp.wait_ge(fw_loaded, 16)
                for m in range(3):
                    sp.wait_ge(w_sem[m], 16)
                return

            def refill(b, m, e):
                sp.wait_ge(hi_done[m], b * 2)
                sp.wait_ge(lo_done[m], b * 2)
                load_unit(sp, e, m)

            refill(1, 0, 1)
            with sp.Fori(1, E - 1) as e:
                refill(e, 1, e)
                refill(e + 1, 0, e + 1)
                refill(e, 2, e)
            for m in (1, 2):
                refill(E - 1, m, E - 1)

            def over(j):
                ex = sp.value_load(over_i[0:1, bass.ds(j, 1)], min_val=0, max_val=E - 1)
                for m in range(3):
                    refill(j + E, m, ex)

            over_loop(sp, over)
            sp.wait_ge(moe_done, 1)
            y_v = y_dram.rearrange("(t k) d -> t (k d)", k=2)

            for t in range(FT):
                sp.dma_start(yf[t], y_v[META + t * 128:META + (t + 1) * 128, :]).then_inc(yf_loaded[t], 16)
            for t in range(FT):
                sp.wait_ge(f_out, t + 1)
                sp.dma_start(out[t * 128:(t + 1) * 128, :], of[t]).then_inc(f_stored, 16)
            sp.wait_ge(f_stored, 16 * FT)

        def tail_tensor(pe):
            def out_tile(u, b, k):
                o, cols = bank[2 * u + b][0:C, :], slice(b * 512, (b + 1) * 512)
                nc.tensor.matmul(o, y_hi[u][:, k, :], w_out_hi[:, k, cols], start=(k == 0), stop=False)
                nc.tensor.matmul(o, y_hi[u][:, k, :], w_out_lo[:, k, cols], start=False, stop=False)
                m = nc.tensor.matmul(o, y_lo[u][:, k, :], w_out_hi[:, k, cols], start=False, stop=(k == KD - 1))
                if k == KD - 1:
                    m.then_inc(out_done, 1)

            def out_half(t, u, b):
                if b == 0:
                    pe.wait_ge(yst_done, t + 1)
                for k in range(KD):
                    out_tile(u, b, k)

            def turn_rows(t, u):
                pe.wait_ge(x2_done, t + 1)
                for b in range(2):
                    for k in range(4):
                        m = nc.tensor.transpose(bank[4 + b][:, k * C:(k + 1) * C],
                                                x2_sb[u][0:C, (4 * b + k) * 128:(4 * b + k + 1) * 128], ident[0:C, 0:C])
                    m.then_inc(tr_done, 1)

            def router(t, u):
                pe.wait_ge(x2T_done, (t + 1) * 2)
                for k in range(KD):
                    m = nc.tensor.matmul(bank[6 + u][0:C, 0:36], x2T[:, k, :], wr[:, k, :], start=(k == 0), stop=(k == KD - 1))
                m.then_inc(lg_ps, 1)

            pe.wait_ge(yst_done, 1)
            for k in range(KD):
                if k % 2 == 0:
                    pe.wait_ge(wo_lo_done, k // 2 + 1)
                for b in range(2):
                    out_tile(0, b, k)
            def chunk(t, u):
                out_half(t, u, 0)
                if not isinstance(t, int) or t > 1:
                    router(t - 2, u)
                out_half(t, u, 1)
                turn_rows(t - 1, 1 - u)

            chunk(1, 1)
            with pe.Fori(1, NC // 2) as i:
                chunk(i * 2, 0)
                chunk(i * 2 + 1, 1)
            router(NC - 2, 0)
            turn_rows(NC - 1, 1)
            router(NC - 1, 1)
            pe.wait_ge(r_dve, RANK_IN)
            flat = lambda a: a[0:C].rearrange("p t e -> p (t e)")
            nc.tensor.matmul(bank[0][0:C, 0:NC * E], strict, flat(ecnt), start=True, stop=False)
            nc.tensor.matmul(bank[0][0:C, 0:NC * E], ones[0:C, 0:C], flat(epre), start=False, stop=True)
            nc.tensor.matmul(bank[1][:, 0:E], ones[0:C, :], tcnt[0:C], start=True, stop=True).then_inc(r_pe, 1)
            pe.wait_ge(r_dve, TABLE_IN)
            for n in range(2 * NC):
                m = nc.tensor.matmul(bank[2][:, 0:3 * BLOCKS], slot1h[0:C, n, :],
                                     vals[0:C, n].rearrange("p a b -> p (a b)"), start=(n == 0), stop=(n == 2 * NC - 1))
            m.then_inc(r_pe, 1)
            if stop == "route":
                return

            def turn(e, p, loads):
                pe.wait_ge(gathered[p], loads)
                for b in range(2):
                    for k in range(4):
                        m = nc.tensor.transpose(bank[5 + b][:, k * 128:(k + 1) * 128],
                                                xg[p][:, (4 * b + k) * 128:(4 * b + k + 1) * 128], ident)
                m.then_inc(xt_e, 1)

            def product(out, hi_lo, k, m, cols, start, stop_):
                kk = KD if m < 2 else 4
                wh, wl = [w[m].rearrange("p (k n) -> p k n", k=kk)[:, k, cols] for w in (w_hi, w_lo)]
                xh, xl = [x[:, k, :] for x in hi_lo]
                nc.tensor.matmul(out, xh, wh, start=start, stop=False)
                nc.tensor.matmul(out, xh, wl, start=False, stop=False)
                return nc.tensor.matmul(out, xl, wh, start=False, stop=stop_)

            def gate_up(e, p, m, tiles):
                for k in tiles:
                    if k % 4 == 0:
                        pe.wait_ge(hi_done[m], e * 2 + k // 4 + 1)
                        pe.wait_ge(lo_done[m], e * 2 + k // 4 + 1)
                        if m == 0:
                            pe.wait_ge(xte_dve, e * 2 + k // 4 + 1)
                    mm = product(bank[p if m == 0 else 2][:, :], xgT[p], k, m, slice(0, FE), k == 0, k == KD - 1)
                if k == KD - 1:
                    mm.then_inc(g_done if m == 0 else u_done, 1)

            def hid_turn(e):
                pe.wait_ge(hid_done, e + 1)
                for k in range(4):
                    m = nc.tensor.transpose(bank[7][:, k * 128:(k + 1) * 128], hid[:, k * 128:(k + 1) * 128], ident)
                m.then_inc(ht_e, 1)

            def down(e):
                pe.wait_ge(hte_done, e + 1)
                for k in range(4):
                    if k % 2 == 0:
                        pe.wait_ge(hi_done[2], e * 2 + k // 2 + 1)
                        pe.wait_ge(lo_done[2], e * 2 + k // 2 + 1)
                    for b in range(2):
                        mm = product(bank[3 + b][:, :], hidT, k, 2, slice(b * 512, (b + 1) * 512), k == 0, k == 3)
                mm.then_inc(d_done, 1)

            lower, upper = range(KD // 2), range(KD // 2, KD)
            turn(0, 0, 16)
            gate_up(0, 0, 0, range(KD))
            turn(1, 1, 16)
            gate_up(0, 0, 1, range(KD))

            def expert(e, p, loads):
                gate_up(e, p, 0, lower)
                hid_turn(e - 1)
                gate_up(e, p, 0, upper)
                down(e - 1)
                if loads is not None:
                    turn(e + 1, 1 - p, loads)
                gate_up(e, p, 1, range(KD))

            with pe.Fori(0, E // 2 - 1) as j:
                expert(j * 2 + 1, 1, j * 16 + 32)
                expert(j * 2 + 2, 0, j * 16 + 32)
            expert(E - 1, 1, None)
            hid_turn(E - 1)
            down(E - 1)

            def over(j):
                turn(j + E, 0, j * 16 + 16 * (E // 2 + 1))
                gate_up(j + E, 0, 0, range(KD))
                gate_up(j + E, 0, 1, range(KD))
                hid_turn(j + E)
                down(j + E)

            over_loop(pe, over)

        def tail_scalar(act):
            act.wait_ge(oy_done, H)
            for m in range(2):
                load_unit(act, 0, m)

            def y_high(u, t):
                cols = slice(t * C, (t + 1) * C) if isinstance(t, int) else bass.ds(t * C, C)
                nc.scalar.activation(y_hi[u], yT[:, :, cols], ACT.Copy).then_inc(y_hi_done, 1)

            y_high(0, 0)
            act.wait_ge(s_wout, 16)
            for q in range(4):
                nc.scalar.activation(w_out_hi[:, 2 * q:2 * q + 2, :], w_out_raw[:, 2 * q:2 * q + 2, :],
                                     ACT.Copy).then_inc(wo_hi_done, 1)
            y_high(1, 1)

            def chunk_ff(u, t, more):
                if more:
                    act.wait_ge(out_done, t * 2 + 2)
                    y_high(u, t + 2)
                act.wait_ge(res_done, (t + 1) * 2)
                nc.scalar.activation(x2_sb[u][0:C, :], h_sb[u][0:C, :], ACT.Square,
                                     accum_out=stat[0:C, u, 0:1]).then_inc(ff_stat, 1)
                act.wait_ge(ff_stat, t * 2 + 1)
                nc.scalar.activation(stat[0:C, u, 1:2], stat[0:C, u, 0:1], ACT.Ln, scale=1.0 / D,
                                     bias=eps[0:C, :]).then_inc(ff_stat, 1)
                act.wait_ge(ff_stat, t * 2 + 2)
                nc.scalar.activation(stat[0:C, u, 2:3], stat[0:C, u, 1:2], ACT.Exp, scale=-0.5).then_inc(ffr_done, 1)
                for b in range(2):
                    act.wait_ge(tr_done, t * 2 + b + 1)
                    nc.scalar.activation(x2T[:, 4 * b:4 * b + 4, :],
                                         bank[4 + b][:, 0:4 * C].rearrange("p (k c) -> p k c", k=4),
                                         ACT.Copy).then_inc(x2T_done, 1)

            with act.Fori(0, NC // 2 - 1) as i:
                for u in range(2):
                    chunk_ff(u, i * 2 + u, True)
            for u in range(2):
                chunk_ff(u, NC - 2 + u, False)
            def split(e, m):
                act.wait_ge(w_sem[m], e * 16 + 16)
                if not isinstance(e, int) or e > 0:
                    act.wait_ge((g_done, u_done, d_done)[m], e)
                for b in range(2):
                    half = slice(b * WU // 2, (b + 1) * WU // 2)
                    nc.scalar.activation(w_hi[m][:, half], wraw[m][:, half], ACT.Copy).then_inc(hi_done[m], 1)

            act.wait_ge(r_dve, GRP_DIFF)
            nc.scalar.activation(grp_v[1][0:C], grp_v[1][0:C], ACT.Exp).then_inc(r_act, 1)
            act.wait_ge(r_dve, TOP_DIFF)
            nc.scalar.activation(tk[4][0:C], tk[4][0:C], ACT.Exp).then_inc(r_act, 1)
            act.wait_ge(h_stored, 16 * NC)
            act.wait_ge(x2_stored, 16 * NC)
            split(0, 0)
            split(0, 1)
            if stop == "route":
                return

            def turned(e, p):
                act.wait_ge(xt_e, e + 1)
                for b in range(2):
                    nc.scalar.activation(xgT[p][0][:, 4 * b:4 * b + 4, :], bank[5 + b][:, :].rearrange("p (k n) -> p k n", k=4),
                                         ACT.Copy).then_inc(xte_act, 1)

            def silu_gate(e, p):
                act.wait_ge(g_done, e + 1)
                nc.scalar.activation(gs[p], bank[p][:, :], ACT.Silu).then_inc(silu_e, 1)

            def down_in(e):
                act.wait_ge(ht_e, e + 1)
                nc.scalar.activation(hidT[0], bank[7][:, :].rearrange("p (k n) -> p k n", k=4), ACT.Copy).then_inc(hta_done, 1)

            def y_out(e, p):
                act.wait_ge(d_done, e + 1)
                act.wait_ge(icol, e + 2)
                for b in range(2):
                    m = nc.scalar.activation(ysb[p][:, b * 512:(b + 1) * 512], bank[3 + b][:, :], ACT.Copy, scale=wcol[p])
                m.then_inc(y_act, 1)

            turned(0, 0)
            silu_gate(0, 0)
            split(1, 0)
            turned(1, 1)
            split(0, 2)

            def expert(e, p):
                split(e, 1)
                down_in(e - 1)
                silu_gate(e, p)
                split(e + 1, 0)
                y_out(e - 1, 1 - p)
                turned(e + 1, 1 - p)
                split(e, 2)

            with act.Fori(0, E // 2 - 1) as j:
                expert(j * 2 + 1, 1)
                expert(j * 2 + 2, 0)
            split(E - 1, 1)
            down_in(E - 2)
            silu_gate(E - 1, 1)
            y_out(E - 2, 0)
            split(E - 1, 2)
            down_in(E - 1)
            y_out(E - 1, 1)

            def over(j):
                for m in range(3):
                    split(j + E, m)
                turned(j + E, 0)
                silu_gate(j + E, 0)
                down_in(j + E)
                y_out(j + E, 0)

            over_loop(act, over)
            act.wait_ge(moe_done, 1)
            for t in range(FT):
                act.dma_start(hf[t], h_dram[META + t * 128:META + (t + 1) * 128, :]).then_inc(hf_loaded[t], 16)
            for t in range(FT):
                u = t % 2
                act.wait_ge(f_add, t + 1)
                nc.scalar.activation(of[t], hf[t], ACT.Square, accum_out=stat[:, u, 0:1]).then_inc(f_stat, 1)
                act.wait_ge(f_stat, 2 * t + 1)
                nc.scalar.activation(stat[:, u, 1:2], stat[:, u, 0:1], ACT.Ln, scale=1.0 / D, bias=eps).then_inc(f_stat, 1)
                act.wait_ge(f_stat, 2 * t + 2)
                nc.scalar.activation(stat[:, u, 2:3], stat[:, u, 1:2], ACT.Exp, scale=-0.5).then_inc(f_rstd, 1)

        def tail_vector(dve):
            def logits_of(t, u):
                dve.wait_ge(lg_ps, t + 1)
                o = logits[0:C, t, :] if isinstance(t, int) else logits[0:C, bass.ds(t, 1), :].rearrange("p o n -> p (o n)")
                nc.vector.tensor_tensor(o, bank[6 + u][0:C, 0:36], param("bias", C), ALU.add).then_inc(lg_done, 1)

            for q in range(4):
                dve.wait_ge(wo_hi_done, q + 1)
                nc.vector.tensor_tensor(w_out_lo[:, 2 * q:2 * q + 2, :], w_out_raw[:, 2 * q:2 * q + 2, :],
                                        w_out_hi[:, 2 * q:2 * q + 2, :].bitcast(F32), ALU.subtract).then_inc(wo_lo_done, 1)
            dve.wait_ge(s_ffw, 16)
            def residual(t, u, loads):
                dve.wait_ge(xr_loaded[u], loads)
                for b in range(2):
                    dve.wait_ge(out_done, t * 2 + b + 1)
                    hs = h_sb[u][0:C, b * 512:(b + 1) * 512]
                    nc.vector.tensor_tensor(hs, bank[2 * u + b][0:C, :], hs, ALU.add).then_inc(res_done, 1)
                dve.wait_ge(ffr_done, t + 1)
                nc.vector.scalar_tensor_tensor(x2_sb[u][0:C, :], h_sb[u][0:C, :], stat[0:C, u, 2:3], ffw[0:C, :],
                                               ALU.mult, ALU.mult).then_inc(x2_done, 1)

            residual(0, 0, 16)
            with dve.Fori(0, NC // 2 - 1) as i:
                residual(i * 2 + 1, 1, i * 16 + 16)
                logits_of(i * 2, 0)
                residual(i * 2 + 2, 0, i * 16 + 32)
                logits_of(i * 2 + 1, 1)
            residual(NC - 1, 1, NC // 2 * 16)
            logits_of(NC - 2, 0)
            logits_of(NC - 1, 1)
            dve.wait_ge(lg_done, NC)

            def split(e, m, halves=(0, 1)):
                for b in halves:
                    half = slice(b * WU // 2, (b + 1) * WU // 2)
                    dve.wait_ge(hi_done[m], e * 2 + b + 1)
                    nc.vector.tensor_tensor(w_lo[m][:, half], wraw[m][:, half], w_hi[m][:, half].bitcast(F32),
                                            ALU.subtract).then_inc(lo_done[m], 1)

            steps = [0]

            def step(ins, wait=True):
                steps[0] += 1
                ins.then_inc(r_dve, 1)
                if wait:
                    dve.wait_ge(r_dve, steps[0])
                return steps[0]

            tt, stt, ts = nc.vector.tensor_tensor, nc.vector.scalar_tensor_tensor, nc.vector.tensor_scalar

            def red(o, i, op):
                return nc.vector.tensor_reduce(o, i, AX_X, op)

            def per(a, n):
                return a.unsqueeze(2).to_broadcast([C, a.shape[1], n])

            def first_max(v, rank_c, best, hot, tmp, n):
                step(red(best, v, ALU.max))
                step(tt(hot, v, per(best, n), ALU.is_equal))
                step(tt(hot, hot, rank_c.unsqueeze(1).to_broadcast([C, NC, n]), ALU.mult))
                step(red(tmp, hot, ALU.max))
                step(tt(hot, hot, per(tmp, n), ALU.is_equal))

            lgt = logits[0:C]
            lg, le = lgt[:, :, 0:NG], lgt[:, :, NG:36].rearrange("p t (g e) -> p t g e", g=NG)
            T = [a[0:C] for a in tk]
            G = [a[0:C] for a in grp_v]
            X = [a[0:C] for a in exp_v]
            first_max(lg, const("r4", C), T[0], G[0], T[1], NG)
            n = step(tt(G[1], lg, per(T[0], NG), ALU.subtract))
            assert n == GRP_DIFF, (n, "GRP_DIFF")
            dve.wait_ge(r_act, 1)
            step(red(T[2], G[1], ALU.add))
            step(nc.vector.reciprocal(T[2], T[2]))
            prod = e3[0:C].rearrange("p t (g e) -> p t g e", g=NG)
            for g in range(NG):
                step(tt(prod[:, :, g, :], le[:, :, g, :], per(G[0][:, :, g], EPG), ALU.mult), wait=g == NG - 1)
            step(tt(X[0], prod[:, :, 0, :], prod[:, :, 1, :], ALU.add), wait=False)
            step(tt(X[1], prod[:, :, 2, :], prod[:, :, 3, :], ALU.add))
            step(tt(X[0], X[0], X[1], ALU.add))
            first_max(X[0], const("r8", C), T[3], X[1], T[1], EPG)
            step(stt(X[2], X[1], -1e30, X[0], ALU.mult, ALU.add))
            first_max(X[2], const("r8", C), T[4], X[3], T[1], EPG)
            n = step(tt(T[4], T[4], T[3], ALU.subtract))
            assert n == TOP_DIFF, (n, "TOP_DIFF")
            dve.wait_ge(r_act, 2)
            wk = tk2[0][0:C].rearrange("p (t k) -> p t k", k=2)
            step(ts(T[5], T[4], 1.0, None, ALU.add))
            step(nc.vector.reciprocal(T[5], T[5]))
            step(tt(wk[:, :, 0], T[5], T[2], ALU.mult))
            step(tt(wk[:, :, 1], wk[:, :, 0], T[4], ALU.mult))
            for k in range(2):
                v = e1h[k][0:C].rearrange("p t (g e) -> p t g e", g=NG)
                for g in range(NG):
                    step(tt(v[:, :, g, :], X[1 + 2 * k], per(G[0][:, :, g], EPG), ALU.mult), wait=k == 1 and g == NG - 1)
            step(tt(ecnt[0:C], e1h[0][0:C], e1h[1][0:C], ALU.add), wait=False)
            step(nc.vector.memset(epre[0:C, 0, :], 0.0))
            for t in range(1, NC):
                step(tt(epre[0:C, t, :], epre[0:C, t - 1, :], ecnt[0:C, t - 1, :], ALU.add))
            n = step(tt(tcnt[0:C], epre[0:C, NC - 1, :], ecnt[0:C, NC - 1, :], ALU.add))
            assert n == RANK_IN, (n, "RANK_IN")
            dve.wait_ge(r_pe, 1)
            step(nc.vector.tensor_copy(oend, bank[1][:, 0:E]))
            step(ts(nover, oend, float(CAP), None, ALU.is_gt))
            for q in range(2, MAXQ + 1):
                step(stt(nover, oend, float(CAP * q), nover, ALU.is_gt, ALU.add))
            step(nc.vector.memset(tcnt, 1.0))
            step(nc.vector.tensor_tensor_scan(oend, tcnt, nover, 0.0, ALU.mult, ALU.add))
            step(tt(obase, oend, nover, ALU.subtract))
            step(tt(ocmp[0:1], oend[0:1].unsqueeze(1).to_broadcast([1, OVER, E]),
                    const("iota", 1)[:, 0:OVER].unsqueeze(2).to_broadcast([1, OVER, E]), ALU.is_le))
            step(red(ofl[0:1, 0:OVER], ocmp[0:1], ALU.add))
            step(ts(ofl[0:1, 0:OVER], ofl[0:1, 0:OVER], float(E - 1), None, ALU.min))
            step(nc.vector.tensor_copy(ofl[0:1, OVER:OVER + 1], oend[0:1, E - 1:E]))
            step(nc.vector.tensor_copy(over_i[0:1, :], ofl[0:1, :]))
            rk, ex, ob, qq = [tk2[n][0:C].rearrange("p (t k) -> p t k", k=2) for n in (1, 2, 3, 4)]
            ei = const("iota", C)[:, 0:E].unsqueeze(1).to_broadcast([C, NC, E])
            obb = obase[0:C].unsqueeze(1).to_broadcast([C, NC, E])
            rank_ps = bank[0][0:C, 0:NC * E].rearrange("p (t e) -> p t e", e=E)
            for k in range(2):
                for dst, v in ((rk, rank_ps), (ex, ei), (ob, obb)):
                    step(tt(e3[0:C], v, e1h[k][0:C], ALU.mult))
                    step(red(dst[:, :, k], e3[0:C], ALU.add))
            F = [tk2[n][0:C] for n in range(8)]
            step(ts(F[4], F[1], float(CAP), None, ALU.is_ge))
            for q in range(2, MAXQ + 1):
                step(stt(F[4], F[1], float(CAP * q), F[4], ALU.is_ge, ALU.add))
            step(stt(F[5], F[4], -float(CAP), F[1], ALU.mult, ALU.add))
            step(tt(F[6], F[3], F[4], ALU.add))
            step(ts(F[6], F[6], float(E - 1), None, ALU.add))
            step(tt(F[6], F[6], F[2], ALU.subtract))
            step(ts(F[7], F[4], 1.0, None, ALU.min))
            step(tt(F[6], F[6], F[7], ALU.mult))
            step(tt(F[6], F[6], F[2], ALU.add))
            step(tt(slot1h[0:C], const("iota", C).unsqueeze(1).to_broadcast([C, 2 * NC, 128]), per(F[5], 128), ALU.is_equal), wait=False)
            step(tt(blk1h[0:C], const("iota", C)[:, 0:BLOCKS].unsqueeze(1).to_broadcast([C, 2 * NC, BLOCKS]),
                    per(F[6], BLOCKS), ALU.is_equal))
            tok = const("tok", C)
            for k in range(2):
                kk = slice(k, 2 * NC, 2)
                step(tt(vals[0:C, kk, 0, :], blk1h[0:C, kk, :], per(tok, BLOCKS), ALU.mult), wait=False)
            step(tt(vals[0:C, :, 1, :], blk1h[0:C], per(const("dst", C), BLOCKS), ALU.mult), wait=False)
            n = step(tt(vals[0:C, :, 2, :], blk1h[0:C], per(F[0], BLOCKS), ALU.mult))
            assert n == TABLE_IN, (n, "TABLE_IN")
            split(0, 0)
            dve.wait_ge(r_pe, 2)
            tab = bank[2][:, 0:3 * BLOCKS].rearrange("p (a b) -> p a b", a=3)
            step(ts(ttab.rearrange("p b a -> p a b"), tab[:, 0:2, :], float(BIG), None, ALU.add))
            step(nc.vector.tensor_copy(itab, ttab))
            nc.vector.tensor_copy(wtab, tab[:, 2, :]).then_inc(tables, 1)
            dve.wait_ge(tables, 1)
            if stop == "route":
                return
            def columns(eg, pg, es, ps):
                if eg is not None:
                    nc.vector.tensor_copy(gi[pg], itab[:, eg, 0:1] if isinstance(eg, int) else
                                          itab[:, bass.ds(eg, 1), 0:1].rearrange("p o n -> p (o n)"))
                if es is not None:
                    b = slice(es, es + 1) if isinstance(es, int) else bass.ds(es, 1)
                    nc.vector.tensor_copy(si[ps], itab[:, b, 1:2].rearrange("p o n -> p (o n)"))
                    m = nc.vector.tensor_copy(wcol[ps], wtab[:, b])
                    m.then_inc(icol, 1)

            columns(0, 0, None, None)
            nc.vector.tensor_copy(gi[1], itab[:, 1, 0:1]).then_inc(icol, 1)

            def turned(e, p):
                for b in range(2):
                    dve.wait_ge(xte_act, e * 2 + b + 1)
                    nc.vector.tensor_tensor(xgT[p][1][:, 4 * b:4 * b + 4, :],
                                            bank[5 + b][:, :].rearrange("p (k n) -> p k n", k=4),
                                            xgT[p][0][:, 4 * b:4 * b + 4, :].bitcast(F32), ALU.subtract).then_inc(xte_dve, 1)

            def hidden(e, p):
                dve.wait_ge(silu_e, e + 1)
                dve.wait_ge(u_done, e + 1)
                nc.vector.tensor_tensor(hid, bank[2][:, :], gs[p], ALU.mult).then_inc(hid_done, 1)

            def down_in(e):
                dve.wait_ge(hta_done, e + 1)
                nc.vector.tensor_tensor(hidT[1], bank[7][:, :].rearrange("p (k n) -> p k n", k=4), hidT[0].bitcast(F32),
                                        ALU.subtract).then_inc(hte_done, 1)

            turned(0, 0)
            nc.vector.tensor_copy(gi[0], itab[:, 2, 0:1]).then_inc(gi2_done, 1)
            split(0, 1)
            split(1, 0)
            turned(1, 1)
            columns(3, 1, 0, 0)
            split(0, 2)
            hidden(0, 0)

            def expert(e, p, before):
                split(e, 1, [0])
                down_in(e - 1)
                split(e, 1, [1])
                split(e + 1, 0)
                turned(e + 1, 1 - p)
                if before is not None:
                    dve.wait_ge(scattered[p], before * 16)
                columns(e + 3, 1 - p, e, p)
                split(e, 2)
                hidden(e, p)

            expert(1, 1, None)
            with dve.Fori(1, E // 2 - 1) as j:
                expert(j * 2, 0, j)
                expert(j * 2 + 1, 1, j)
            expert(E - 2, 0, E // 2 - 1)
            split(E - 1, 1)
            down_in(E - 2)
            split(E - 1, 2)
            dve.wait_ge(scattered[1], (E // 2 - 1) * 16)
            columns(None, None, E - 1, 1)
            hidden(E - 1, 1)
            down_in(E - 1)

            def over(j):
                dve.wait_ge(scattered[0], (j + E // 2) * 16)
                dve.wait_ge(scattered[1], E // 2 * 16)
                columns(j + E, 0, j + E, 0)
                for m in range(3):
                    split(j + E, m)
                turned(j + E, 0)
                hidden(j + E, 0)
                down_in(j + E)

            over_loop(dve, over)
            dve.wait_ge(fw_loaded, 16)
            for t in range(FT + 1):
                if t < FT:
                    dve.wait_ge(hf_loaded[t], 16)
                    dve.wait_ge(yf_loaded[t], 16)
                    nc.vector.tensor_tensor(hf[t], hf[t], yf[t][:, 0:D], ALU.add).then_inc(f_sum, 1)
                    dve.wait_ge(f_sum, t + 1)
                    nc.vector.tensor_tensor(hf[t], hf[t], yf[t][:, D:2 * D], ALU.add).then_inc(f_add, 1)
                if t:
                    dve.wait_ge(f_rstd, t)
                    nc.vector.scalar_tensor_tensor(of[t - 1], hf[t - 1], stat[:, (t - 1) % 2, 2:3], fw, ALU.mult,
                                                   ALU.mult).then_inc(f_out, 1)

        def tail_pool(pool):
            last_row, last_choice = pool.to_reg(L - 1), pool.to_reg(2 * L - 1)
            pool.wait_ge(oy_done, H)

            def y_low(t, u):
                cols = slice(t * C, (t + 1) * C) if isinstance(t, int) else bass.ds(t * C, C)
                pool.wait_ge(y_hi_done, t + 1)
                nc.gpsimd.tensor_tensor(y_lo[u], yT[:, :, cols], y_hi[u].bitcast(F32), ALU.subtract).then_inc(yst_done, 1)

            y_low(0, 0)
            y_low(1, 1)
            with pool.Fori(0, NC // 2 - 1) as i:
                for u in range(2):
                    pool.wait_ge(out_done, i * 4 + 2 * u + 2)
                    y_low(i * 2 + u + 2, u)
            if stop == "route":
                return

            def gather(p):
                nc.gpsimd.indirect_dma_start(out=xg[p], out_offset=None, in_=xn_dram,
                                             in_offset=bass.IndirectOffsetOnAxis(ap=gi[p], axis=0),
                                             bounds_check=last_row, oob_is_err=False).then_inc(gathered[p], 16)

            def scatter(e, p):
                pool.wait_ge(icol, e + 2)
                pool.wait_ge(y_act, e + 1)
                nc.gpsimd.indirect_dma_start(out=y_dram, out_offset=bass.IndirectOffsetOnAxis(ap=si[p], axis=0),
                                             in_=ysb[p], in_offset=None,
                                             bounds_check=last_choice, oob_is_err=False).then_inc(scattered[p], 16)

            pool.wait_ge(out_done, 2 * NC)
            for p in range(2):
                nc.gpsimd.memset(xg[p], 0.0).then_inc(xg_zero, 1)
            pool.wait_ge(xg_zero, 2)
            pool.wait_ge(x2_stored, 16 * NC)
            pool.wait_ge(icol, 1)
            gather(0)
            gather(1)
            pool.wait_ge(gi2_done, 1)
            pool.wait_ge(xte_act, 1)
            gather(0)
            for e in range(E):
                if e + 3 < E:
                    pool.wait_ge(icol, e + 2)
                    gather((e + 3) % 2)
                scatter(e, e % 2)
            for p in range(2):
                pool.wait_ge(scattered[p], E // 2 * 16)
            total = pool.value_load(over_i[0:1, OVER:OVER + 1], min_val=0, max_val=OVER)
            for j in range(OVER):
                with pool.If(total > j):
                    pool.wait_ge(icol, j + E + 2)
                    gather(0)
                    scatter(j + E, 0)
                    pool.wait_ge(scattered[0], (j + E // 2 + 1) * 16)
            nc.gpsimd.memset(stat[0:1, 0, 3:4], 0.0).then_inc(moe_done, 1)

        block = ctx.enter_context(nc.Block())

        def tile_done(h, kind, pieces=3):
            return h * 21 + 9 + 3 * kind + pieces

        ACT_ORDER = [Z, GC, Q, K, V]

        def by_act(h, kind, pieces=3):
            return h * 15 + 9 + 3 * ACT_ORDER.index(kind) + pieces

        def by_dve(h, kind, pieces=3):
            return h * 6 + 3 * (kind - UU) + pieces

        ROUNDS = ["grow", "vtr", "ktr", "gk", "gq", "mtr", "ttr0"]
        for n in range(1, LEVELS):
            ROUNDS += [f"z{n}", f"rz{n}"] + ([f"ttr{n}"] if n < LEVELS - 1 else [])
        DVE_R = [r for r in ROUNDS if r in ("grow", "vtr", "ktr", "gk", "gq", "mtr") or r.startswith("rz")]
        ACT_R = [r for r in ROUNDS if r == "grow" or r not in DVE_R]

        def at(order, h, name, g):
            return h * (3 * len(order)) + 3 * order.index(name) + g + 1

        SUMS = ["mix", "o", "q", "k"]

        def sums(h, name, pieces=3):
            return h * 12 + 6 + 3 * SUMS.index(name) + pieces

        def chunk(a, c):
            return a[:, c * C:(c + 1) * C]

        def bmat(g, w=C):
            n = len(GROUPS[g])
            return bank[3 + g][:, 0:n * w].rearrange("p (a b) -> p a b", a=n)

        def gsl(g):
            return slice(GROUPS[g].start, GROUPS[g].stop)

        @block.sync
        def _(sp):
            def load_x(t):
                sp.dma_start(x_sb[t][0:C, :], x[t * C:(t + 1) * C, :]).then_inc(x_loaded[t % NB], 16)

            load_x(0)
            sp.dma_start(const_sb, consts).then_inc(s_const, 16)
            sp.dma_start(par_sb, par).then_inc(s_const, 16)
            for t in range(1, NB):
                load_x(t)
            for t in range(NB, NC):
                sp.wait_ge(x_loaded[t - NB], 16)
                load_x(t)
            for s, kind in ((0, Q), (1, K), (2, V), (3, KINDS + GB)):
                n = s if s < 3 else 3 + GB
                sp.dma_start(wst[s], wt[n].rearrange("p (k n) -> p k n", k=KD)).then_inc(w_loaded[s], 16)
            def load_w(s, n):
                sp.dma_start(wst[s], wt[bass.ds(n, 1)].rearrange("o p (k n) -> (o p) k n", k=KD)
                             if not isinstance(n, int) else wt[n].rearrange("p (k n) -> p k n", k=KD)
                             ).then_inc(w_loaded[s], 16)

            for s in range(3):
                sp.wait_ge(proj_done, 3 * (s + 1))
                load_w(s, 3 + s)
            with sp.Fori(0, H - 1) as h:
                for s in range(3):
                    sp.wait_ge(proj_done, tile_done(h, s))
                    load_w(s, h * 7 + 3 + Q + s)
                sp.wait_ge(proj_done, tile_done(h, GB))
                load_w(3, h * 7 + 10 + GB)
                for s in range(3):
                    sp.wait_ge(proj_done, tile_done(h, Q + s))
                    load_w(s, h * 7 + 10 + s)
            h = H - 1
            sp.wait_ge(proj_done, tile_done(h, GB))
            sp.dma_start(w_out_raw, w_out.rearrange("(k p) n -> p k n", p=128)).then_inc(s_wout, 16)
            if stop == "mixer":
                return
            tail_sync(sp)

        def project(pe, kind, pc, slot, tiles=range(KD)):
            o, n = PIECE[pc]
            for k in tiles:
                m = nc.tensor.matmul(bank[pc][:, 0:n], wst[slot][:, k, :], xnT[:, k, o:o + n],
                                     start=(k == 0), stop=(k == KD - 1))
            if k == KD - 1:
                m.then_inc(proj_done, 1)

        def sum_pieces(pe, h, name, src, mat, first=0):
            base = first + 3 * (SUMS.index(name) if h is not None else 0)
            for pc, (o, n) in enumerate(PIECE):
                b = 6 + (base + pc) % 2
                if h is None:
                    if base + pc >= 2:
                        pe.wait_ge(sum_act, base + pc - 1)
                else:
                    pe.wait_ge(sum_act, sums(h, name, pc - 1))
                nc.tensor.matmul(bank[b][:, 0:n], mat, src[:, o:o + n], start=True, stop=True).then_inc(sum_done, 1)

        @block.tensor
        def _(pe):
            pe.wait_ge(s_const, 32)
            for t in range(NC):
                pe.wait_ge(xn_done, t + 1)
                if t >= 4:
                    pe.wait_ge(xnT_done, 2 * (t - 3))
                for b in range(2):
                    for k in range(4):
                        m = nc.tensor.transpose(bank[2 * (t % 4) + b][:, k * C:(k + 1) * C],
                                                xn_sb[t % NB][0:C, (4 * b + k) * 128:(4 * b + k + 1) * 128],
                                                ident[0:C, 0:C])
                    m.then_inc(xt_done, 1)
            pe.wait_ge(xnT_done, 2 * NC)
            for s in range(3):
                pe.wait_ge(w_loaded[s], 16)
                for pc in range(3):
                    if s:
                        pe.wait_ge(proj_act, 3 * (s - 1) + pc + 1)
                    project(pe, Q + s, pc, s)
            for c in range(NC):
                for k in range(KD):
                    m = nc.tensor.matmul(bank[7][0:C, c * 8:c * 8 + 8], xnT[:, k, c * C:(c + 1) * C], wab[:, k, :],
                                         start=(k == 0), stop=(k == KD - 1))
            m.then_inc(ab_done, 1)
            pe.wait_ge(gt_done, 1)
            gf = g_tok[0:C].rearrange("p h c -> p (h c)")
            nc.tensor.matmul(bank[6][0:C, 0:40], incl, gf, start=True, stop=True)
            nc.tensor.matmul(bank[6][:, 64:104], ones[0:C, :], gf, start=True, stop=True).then_inc(gsum_done, 1)
            pe.wait_ge(gates_dve, 6)
            pe.wait_ge(gates_act, 6)
            for n, s in enumerate(("q", "k")):
                pe.wait_ge(sq_done, n + 1)
                sum_pieces(pe, None, s, sq[n], ones, first=3 * n)

            def fill(h, kind, pc, tiles=range(KD)):
                s = kind % 4 if kind < Q else kind - Q
                if tiles[0] > 0:
                    project(pe, kind, pc, s, tiles)
                    return
                if pc == 0:
                    pe.wait_ge(w_loaded[s], (h + 1) * 16 if kind == GB else
                               (h * 2 + (2 if kind < GB else 3)) * 16)
                if kind == Z:
                    pe.wait_ge(proj_act, h * 15 + 6 + pc + 1)
                elif kind in (GC, UU):
                    pe.wait_ge(proj_act, by_act(h, kind - 1, pc + 1))
                elif kind in (GB, Q):
                    pe.wait_ge(proj_dve, by_dve(h, kind - 1, pc + 1))
                else:
                    pe.wait_ge(proj_act, by_act(h, kind - 1, pc + 1))
                project(pe, kind, pc, s, tiles)

            def rnd(h, name):
                prev = ROUNDS[ROUNDS.index(name) - 1] if name != "grow" else None
                for g in range(3):
                    if prev in ACT_R:
                        pe.wait_ge(gdn_act, at(ACT_R, h, prev, g))
                    if prev in DVE_R:
                        pe.wait_ge(gdn_dve, at(DVE_R, h, prev, g))
                    if name.startswith("z") and g == 0:
                        pe.wait_ge(a_done, h * LEVELS + int(name[1:]) + 1)
                    if name == "ttr0" and g == 0:
                        pe.wait_ge(t0_done, h + 1)
                    if name == "vtr" and g == 0:
                        pe.wait_ge(silu_done, h * 3 + 3)
                    if name == "ktr" and g == 0:
                        pe.wait_ge(qk_done, h * 2 + 2)
                    if name == "grow" and g == 0:
                        pe.wait_ge(head_done, h + 1)
                    if name.startswith("rz") and name != "rz1":
                        pe.wait_ge(gdn_act, at(ACT_R, h, "ttr" + str(int(name[2:]) - 1), g))
                    for n, c in enumerate(GROUPS[g]):
                        o = bmat(g)[0:C, n, :]
                        if name == "grow":
                            m = nc.tensor.matmul(bmat(g)[:, n, :], gbc[0:C, c, :], incl, start=True, stop=True)
                        elif name in ("vtr", "ktr"):
                            m = nc.tensor.transpose(bmat(g, 128)[0:C, n, :], chunk(vT if name == "vtr" else kT, c), ident)
                        elif name in ("gk", "gq"):
                            m = nc.tensor.matmul(o, chunk(kT, c), chunk(kT if name == "gk" else qT, c),
                                                 start=True, stop=True)
                        elif name == "mtr":
                            m = nc.tensor.transpose(o, mT[0:C, c, :], ident[0:C, 0:C])
                        elif name == "ttr0":
                            m = nc.tensor.transpose(o, tI[0:C, c, :], ident[0:C, 0:C])
                        elif name.startswith("ttr"):
                            m = nc.tensor.transpose(o, rT[0:C, c, :], ident[0:C, 0:C])
                        elif name.startswith("rz"):
                            m = nc.tensor.matmul(o, tI[0:C, c, :], zz[0:C, c, :], start=True, stop=True)
                        else:
                            m = nc.tensor.matmul(o, aL[int(name[1:]) % 2][0:C, c, :], rT[0:C, c, :],
                                                 start=True, stop=True)
                    m.then_inc(gdn_done, 1)

            def scan(h, last):
                pe.wait_ge(sum_act, sums(h, "mix"))
                pe.wait_ge(qg_done, h + 1)
                for g in range(3):
                    pe.wait_ge(gdn_dve, at(DVE_R, h, "rz" + str(LEVELS - 1), g))
                for c in range(NC):
                    pe.wait_ge(s_done, h * (NC + 1) + c + 1)
                    nc.tensor.matmul(bank[3][0:C, 0:128], chunk(kT, c), state, start=True, stop=True).then_inc(ks_done, 1)
                    if not last and c < 9:
                        fill(h, Q + c // 3, c % 3, range(0, 3))
                    if c:
                        pe.wait_ge(o_done, h * NC + c)
                    nc.tensor.matmul(bank[5][:, 0:C], state, chunk(qg, c), start=True, stop=False)
                    pe.wait_ge(r_done, h * NC + c + 1)
                    nc.tensor.matmul(bank[4][0:C, 0:128], rT[0:C, c, :], r_sb[0:C, :],
                                     start=True, stop=True).then_inc(vnp_done, 1)
                    if not last and c < 9:
                        fill(h, Q + c // 3, c % 3, range(3, 6))
                    pe.wait_ge(vn_done, h * NC + c + 1)
                    nc.tensor.matmul(bank[5][:, 0:C], vn_sb[0:C, :], dTi[0:C, c, :], start=False, stop=True)
                    nc.tensor.matmul(bank[6][:, 0:128], kd[0:C, c, :], vn_sb[0:C, :],
                                     start=True, stop=True).then_inc(ods_done, 1)
                    if not last and c < 9:
                        fill(h, Q + c // 3, c % 3, range(6, 8))
                pe.wait_ge(s_done, h * (NC + 1) + NC + 1)
                pe.wait_ge(o_done, h * NC + NC)

            def mixer(h, last):
                rnd(h, "grow")
                fill(h, Z, 2)
                rnd(h, "vtr")
                rnd(h, "ktr")
                fill(h, GC, 0)
                rnd(h, "gk")
                fill(h, GC, 1)
                rnd(h, "gq")
                rnd(h, "mtr")
                fill(h, GC, 2)
                rnd(h, "ttr0")
                fills = [(UU, 0), (UU, 1), (UU, 2), (GB, 0), (GB, 1), (GB, 2)]
                for n in range(1, LEVELS):
                    rnd(h, f"z{n}")
                    if fills:
                        fill(h, *fills.pop(0))
                    rnd(h, f"rz{n}")
                    if fills:
                        fill(h, *fills.pop(0))
                    if n == 5:
                        pe.wait_ge(sq_done, h * 4 + 3)
                        sum_pieces(pe, h, "mix", sq[0], bones)
                    if n < LEVELS - 1:
                        rnd(h, f"ttr{n}")
                scan(h, last)
                if not last:
                    fill(h + 1, Z, 0)
                pe.wait_ge(sq_done, h * 4 + (5 if not last else 4))
                sum_pieces(pe, h, "o", sq[1], ones)
                if not last:
                    sum_pieces(pe, h, "q", sq[0], ones)
                    fill(h + 1, Z, 1)
                    pe.wait_ge(sq_done, h * 4 + 6)
                    sum_pieces(pe, h, "k", sq[1], ones)

            fill(0, Z, 0)
            fill(0, Z, 1)
            with pe.Fori(0, H - 1) as h:
                mixer(h, False)
            mixer(H - 1, True)
            if stop == "mixer":
                return
            tail_tensor(pe)

        @block.scalar
        def _(act):
            act.wait_ge(s_const, 32)
            for b in range(2):
                for t in range(b * NB, (b + 1) * NB):
                    act.wait_ge(x_loaded[t % NB], 16 * (b + 1))
                    if t:
                        act.wait_ge(ss_done, t + b)
                    nc.scalar.activation(junk[0:C, :], x_sb[t][0:C, :], ACT.Square,
                                         accum_out=nstat[0:C, 0, t:t + 1]).then_inc(ss_done, 1)
                tiles = slice(b * NB, (b + 1) * NB)
                act.wait_ge(ss_done, (b + 1) * NB + b)
                nc.scalar.activation(nstat[0:C, 1, tiles], nstat[0:C, 0, tiles], ACT.Ln, scale=1.0 / D,
                                     bias=eps[0:C, :]).then_inc(ss_done, 1)
                act.wait_ge(ss_done, (b + 1) * (NB + 1))
                nc.scalar.activation(nstat[0:C, 2, tiles], nstat[0:C, 1, tiles], ACT.Exp, scale=-0.5).then_inc(rstd_done, 1)
            act.wait_ge(zeros_done, 2)

            def evac_raw(pc, buf):
                o, n = PIECE[pc]
                nc.scalar.activation(raw[buf][:, 3 + o:3 + o + n], bank[pc][:, 0:n], ACT.Copy).then_inc(proj_act, 1)

            def silu(dst, n):
                nc.scalar.activation(dst, cv[n], ACT.Silu).then_inc(silu_done, 1)

            def norm(first, count, buf, scale, shift):
                for pc, (o, n) in enumerate(PIECE):
                    act.wait_ge(sum_done, count(pc + 1))
                    nc.scalar.activation(rs[buf][:, o:o + n], bank[6 + (first + pc) % 2][:, 0:n], ACT.Ln,
                                         scale=scale, bias=eps).then_inc(sum_act, 1)
                act.wait_ge(sum_act, count(3))
                kw = {"bias": shift} if shift is not None else {}
                nc.scalar.activation(rs[buf], rs[buf], ACT.Exp, scale=-0.5, **kw).then_inc(rs_done, 1)

            qb = const("qb")
            for s in range(3):
                if s == 2:
                    act.wait_ge(conv_step, 4)
                for pc in range(3):
                    act.wait_ge(proj_done, 3 * s + pc + 1)
                    evac_raw(pc, s % 2)
            for s, dst in enumerate((cv[0], cv[1], vT)):
                act.wait_ge(conv_step, 4 * s + 4)
                silu(dst, s)
            ab = bank[7][0:C, 0:80].rearrange("p (c n) -> p n c", n=8)
            act.wait_ge(gates_dve, 1)
            nc.scalar.activation(small[0:C, 1, :], small[0:C, 1, :], ACT.Exp, scale=-1.0).then_inc(gates_act, 1)
            nc.scalar.activation(ea[0:C, :], param("alog", C), ACT.Exp).then_inc(gates_act, 1)
            nc.scalar.activation(small[0:C, 2, :].rearrange("p (h c) -> p h c", h=H), ab[:, 4:8, :], ACT.Exp,
                                 scale=-1.0).then_inc(gates_act, 1)
            act.wait_ge(gates_act, 3)
            nc.scalar.activation(small[0:C, 1, :], small[0:C, 1, :], ACT.Ln, bias=1.0).then_inc(gates_act, 1)
            act.wait_ge(gates_dve, 6)
            nc.scalar.activation(small[0:C, 3, :], bank[6][0:C, 0:40], ACT.Exp).then_inc(gates_act, 1)
            nc.scalar.activation(a_last.rearrange("p h c -> p (h c)"), bank[6][:, 64:104], ACT.Exp).then_inc(gates_act, 1)
            nc.scalar.activation(tok_sc[0:C, :, 3, :], tok_sc[0:C, :, 3, :], ACT.Exp).then_inc(gates_act, 1)
            norm(0, lambda p: p, 0, 1.0, qb)
            norm(3, lambda p: 3 + p, 1, 1.0, None)

            def grp(h, name, dst, func):
                for g in range(3):
                    act.wait_ge(gdn_done, at(ROUNDS, h, name, g))
                    n = len(GROUPS[g])
                    if name == "grow":
                        act.wait_ge(gdn_dve, at(DVE_R, h, name, g))
                        nc.scalar.activation(eG[:, GROUPS[g].start * C:GROUPS[g].stop * C], bank[3 + g][:, 0:n * C],
                                             func).then_inc(gdn_act, 1)
                    else:
                        nc.scalar.activation(dst[0:C, gsl(g), :], bmat(g)[0:C], func).then_inc(gdn_act, 1)

            def mixer(h, last):
                grp(h, "grow", None, ACT.Exp)
                act.wait_ge(gdn_dve, at(DVE_R, h, "grow", 2))
                nc.scalar.activation(dT[0:C], dT[0:C], ACT.Exp).then_inc(dexp_done, 1)
                for pc, (o, n) in enumerate(PIECE):
                    act.wait_ge(proj_done, tile_done(h, Z, pc + 1))
                    nc.scalar.activation(zs[:, o:o + n], bank[pc][:, 0:n], ACT.Silu).then_inc(proj_act, 1)
                for pc in range(3):
                    act.wait_ge(proj_done, tile_done(h, GC, pc + 1))
                    evac_raw(pc, 0)
                grp(h, "ttr0", rT, ACT.Copy)
                for n in range(1, LEVELS):
                    grp(h, f"z{n}", zz, ACT.Copy)
                    if n == 5:
                        norm(0, lambda p: sums(h, "mix", p), 0, 1.0 / 64, None)
                    if n < LEVELS - 1:
                        grp(h, f"ttr{n}", tI, ACT.Copy)
                for c in range(NC):
                    act.wait_ge(vnp_done, h * NC + c + 1)
                    nc.scalar.activation(vn_sb[0:C, :], bank[4][0:C, 0:128], ACT.Copy).then_inc(vn_done, 1)
                    act.wait_ge(ods_done, h * NC + c + 1)
                    nc.scalar.activation(chunk(oT, c), bank[5][:, 0:C], ACT.Copy).then_inc(o_done, 1)
                    if not last and c < 9:
                        act.wait_ge(proj_done, tile_done(h, Q + c // 3, c % 3 + 1))
                        if c == 6:
                            act.wait_ge(conv_step, h * 15 + 19)
                        evac_raw(c % 3, (c // 3) % 2)
                    if not last and c == 6:
                        act.wait_ge(conv_step, h * 15 + 19)
                        silu(cv[0], 0)
                if not last:
                    act.wait_ge(conv_step, h * 15 + 23)
                    silu(cv[1], 1)
                    act.wait_ge(conv_step, h * 15 + 27)
                    silu(vT, 2)
                norm(1, lambda p: sums(h, "o", p), 1, 1.0 / 128, None)
                if not last:
                    act.wait_ge(mixy_done, h + 1)
                    norm(0, lambda p: sums(h, "q", p), 0, 1.0, qb)
                    act.wait_ge(oy_part, h + 1)
                    norm(1, lambda p: sums(h, "k", p), 1, 1.0, None)

            with act.Fori(0, H - 1) as h:
                mixer(h, False)
            mixer(H - 1, True)
            if stop == "mixer":
                return
            tail_scalar(act)

        @block.vector
        def _(dve):
            for u in range(2):
                nc.vector.memset(raw[u][:, 0:3], 0.0).then_inc(zeros_done, 1)
            dve.wait_ge(s_const, 32)
            mw = mixw.unsqueeze(2).to_broadcast([128, KD, C])
            for t in range(NC + 1):
                if t < NC:
                    dve.wait_ge(rstd_done, t // NB + 1)
                    if t >= NB:
                        dve.wait_ge(xt_done, 2 * (t - NB + 1))
                    nc.vector.tensor_scalar(xn_sb[t % NB][0:C, :], x_sb[t][0:C, :], nstat[0:C, 2, t:t + 1], None,
                                            ALU.mult).then_inc(xn_done, 1)
                if t:
                    for b in range(2):
                        dve.wait_ge(xt_done, 2 * (t - 1) + b + 1)
                        nc.vector.tensor_tensor(xnT[:, 4 * b:4 * b + 4, (t - 1) * C:t * C],
                                                bank[2 * ((t - 1) % 4) + b][:, 0:4 * C].rearrange("p (k c) -> p k c", k=4),
                                                mw[:, 4 * b:4 * b + 4, :], ALU.mult).then_inc(xnT_done, 1)

            def conv(n, buf, taps_n, ntap, base):
                dst = cv[n]
                for j in range(ntap):
                    src = raw[buf][:, 4 - ntap + j:4 - ntap + j + L]
                    t = taps[:, taps_n + j:taps_n + j + 1]
                    if j:
                        dve.wait_ge(conv_step, base + j)
                        m = nc.vector.scalar_tensor_tensor(dst, src, t, dst, ALU.mult, ALU.add)
                    else:
                        m = nc.vector.tensor_scalar(dst, src, t, None, ALU.mult)
                    m.then_inc(conv_step, 1)
                    yield

            nc.vector.tensor_copy(taps, taps_all[:, 0:16]).then_inc(taps_done, 1)
            dve.wait_ge(taps_done, 1)
            for s in range(3):
                dve.wait_ge(proj_act, 3 * s + 3)
                for _ in conv(s, s % 2, 4 * s, 4, 4 * s):
                    pass

            ab = bank[7][0:C, 0:80].rearrange("p (c n) -> p n c", n=8)
            t = [small[0:C, n, :].rearrange("p (h c) -> p h c", h=H) for n in range(4)]
            dve.wait_ge(ab_done, 1)
            nc.vector.tensor_tensor(t[0], ab[:, 0:4, :], param("dt", C).unsqueeze(2).to_broadcast([C, H, NC]),
                                    ALU.add).then_inc(adt_done, 1)
            dve.wait_ge(adt_done, 1)
            nc.vector.scalar_tensor_tensor(t[1], t[0], -1.0, t[0], ALU.mult, ALU.max).then_inc(gates_dve, 1)
            dve.wait_ge(gates_act, 4)
            nc.vector.scalar_tensor_tensor(t[0], t[0], 0.0, t[1], ALU.max, ALU.add).then_inc(gates_dve, 1)
            nc.vector.tensor_scalar(t[2], t[2], 1.0, None, ALU.add).then_inc(gates_dve, 1)
            dve.wait_ge(gates_dve, 3)
            nc.vector.scalar_tensor_tensor(g_tok[0:C], t[0], -1.0, ea[0:C].unsqueeze(2).to_broadcast([C, H, NC]),
                                           ALU.mult, ALU.mult).then_inc(gt_done, 1)
            nc.vector.reciprocal(tok_sc[0:C, :, 1, :], t[2]).then_inc(gates_dve, 1)
            dve.wait_ge(gsum_done, 1)
            gc_ps = bank[6][0:C, 0:40].rearrange("p (h c) -> p h c", h=H)
            gl_ps = bank[6][0:C, 64:104].rearrange("p (h c) -> p h c", h=H)
            nc.vector.tensor_copy(tok_sc[0:C, :, 0, :], gc_ps).then_inc(gates_dve, 1)
            dve.wait_ge(gates_dve, 5)
            nc.vector.tensor_tensor(tok_sc[0:C, :, 3, :], gl_ps, tok_sc[0:C, :, 0, :], ALU.subtract).then_inc(gates_dve, 1)
            dve.wait_ge(gates_act, 5)
            nc.vector.scalar_tensor_tensor(tok_sc[0:C, :, 2, :], tok_sc[0:C, :, 1, :], -1.0, t[3], ALU.mult,
                                           ALU.mult).then_inc(gates_dve, 1)

            def head_copies(h):
                dve.wait_ge(gates_dve, 7)
                dve.wait_ge(gates_act, 7)
                hh = slice(h, h + 1) if isinstance(h, int) else bass.ds(h, 1)
                nc.vector.tensor_copy(head_sc[0:C].rearrange("p (o k) c -> p o k c", o=1), tok_sc[0:C, hh])
                nc.vector.tensor_copy(head_a.rearrange("p (o c) -> p o c", o=1), a_last[:, hh])
                nc.vector.tensor_copy(gbc[0:C].rearrange("p (o c) n -> p (o c) n", o=1),
                                      g_tok[0:C, hh].rearrange("p o c -> p (o c)").unsqueeze(2).to_broadcast([C, NC, 128])
                                      ).then_inc(head_done, 1)

            def q_or_k(n, count):
                dve.wait_ge(rs_done, count)
                nc.vector.tensor_tensor((qT, kT)[n], cv[n], rs[n], ALU.mult).then_inc(qk_done, 1)

            head_copies(0)
            q_or_k(0, 1)
            q_or_k(1, 2)

            def grp(h, name):
                for g in range(3):
                    dve.wait_ge(gdn_done, at(ROUNDS, h, name, g))
                    s, n = gsl(g), len(GROUPS[g])

                    def per_token(kind, w):
                        return head_sc[0:C, kind, s].unsqueeze(2).to_broadcast([C, n, w])

                    if name == "grow":
                        nc.vector.tensor_tensor(dT[0:C, s], bmat(g)[0:C], per_token(0, C), ALU.subtract).then_inc(dt_sub, 1)
                        dve.wait_ge(dt_sub, h * 3 + g + 1)
                        m = nc.vector.tensor_scalar(dT[0:C, s], dT[0:C, s], 0.0, None, ALU.min)
                    elif name == "vtr":
                        m = nc.vector.tensor_tensor(bv[0:C, s], bmat(g, 128)[0:C], per_token(1, 128), ALU.mult)
                    elif name == "ktr":
                        m = nc.vector.tensor_tensor(kd[0:C, s], bmat(g, 128)[0:C], per_token(3, 128), ALU.mult)
                    elif name == "gk":
                        m = nc.vector.tensor_tensor(mT[0:C, s], bmat(g)[0:C], dTs[0:C, s], ALU.mult)
                    elif name == "gq":
                        m = nc.vector.tensor_tensor(dTi[0:C, s], bmat(g)[0:C], dTi[0:C, s], ALU.mult)
                    elif name == "mtr":
                        m = nc.vector.tensor_tensor(lM[0:C, s], bmat(g)[0:C], per_token(1, C), ALU.mult)
                    else:
                        m = nc.vector.tensor_tensor(rT[0:C, s], rT[0:C, s], bmat(g)[0:C], ALU.subtract)
                    m.then_inc(gdn_dve, 1)

            def mixer(h, last):
                nc.vector.memset(state, 0.0).then_inc(s_done, 1)
                hn = slice((h + 1) * 16, (h + 2) * 16) if isinstance(h, int) else bass.ds((h + 1) * 16, 16)
                nc.vector.tensor_copy(taps, taps_all[:, hn]).then_inc(taps_done, 1)
                dve.wait_ge(head_done, h + 1)
                grp(h, "grow")
                dve.wait_ge(dexp_done, h + 1)
                nc.vector.tensor_tensor(dTi[0:C], dT[0:C], incl.unsqueeze(1).to_broadcast([C, NC, C]),
                                        ALU.mult).then_inc(dti_done, 1)
                grp(h, "vtr")
                grp(h, "ktr")
                dve.wait_ge(dts_done, h + 1)
                grp(h, "gk")
                dve.wait_ge(dti_done, h + 1)
                grp(h, "gq")
                grp(h, "mtr")

                def u_piece(pc):
                    o, n = PIECE[pc]
                    dve.wait_ge(proj_done, tile_done(h, UU, pc + 1))
                    dve.wait_ge(proj_act, by_act(h, GC, pc + 1))
                    nc.vector.tensor_tensor(raw[1][:, 3 + o:3 + o + n], bank[pc][:, 0:n], raw[0][:, 3 + o:3 + o + n],
                                            ALU.mult).then_inc(proj_dve, 1)

                def gb_piece(pc):
                    o, n = PIECE[pc]
                    dve.wait_ge(proj_done, tile_done(h, GB, pc + 1))
                    nc.vector.tensor_tensor(cv[0][:, o:o + n], bank[pc][:, 0:n], cv[0][:, o:o + n],
                                            ALU.mult).then_inc(proj_dve, 1)

                u_piece(0)
                grp(h, "rz1")
                u_piece(1)
                u_piece(2)
                grp(h, "rz2")
                dve.wait_ge(proj_dve, by_dve(h, UU))
                dve.wait_ge(taps_done, h + 2)
                for _ in conv(0, 1, 12, 3, h * 15 + 12):
                    pass
                dve.wait_ge(conv_step, h * 15 + 15)
                gb_piece(0)
                gb_piece(1)
                grp(h, "rz3")
                gb_piece(2)
                grp(h, "rz4")
                grp(h, "rz5")
                dve.wait_ge(rs_done, h * 4 + 3)
                yh = slice(h, h + 1) if isinstance(h, int) else bass.ds(h, 1)
                nc.vector.scalar_tensor_tensor(yT[:, yh].rearrange("p o l -> p (o l)"), cv[0], taps[:, 15:16], rs[0],
                                               ALU.mult, ALU.mult).then_inc(mixy_done, 1)
                grp(h, "rz6")

                todo = []
                if not last:
                    base = h * 15 + 15
                    todo = [conv(0, 0, 0, 4, base), conv(1, 1, 4, 4, base + 4)]
                for c in range(NC):
                    dve.wait_ge(ks_done, h * NC + c + 1)
                    nc.vector.scalar_tensor_tensor(r_sb[0:C, :], bank[3][0:C, 0:128], head_sc[0:C, 2, c:c + 1],
                                                   bv[0:C, c, :], ALU.mult, ALU.add).then_inc(r_done, 1)
                    dve.wait_ge(ods_done, h * NC + c + 1)
                    nc.vector.scalar_tensor_tensor(state, state, head_a[:, c:c + 1], bank[6][:, 0:128], ALU.mult,
                                                   ALU.add).then_inc(s_done, 1)
                    if not last and c in (3, 4, 6, 7):
                        if c in (3, 6):
                            dve.wait_ge(proj_act, by_act(h, Q if c == 3 else K))
                        for _ in range(2):
                            next(todo[c // 6])
                if not last:
                    dve.wait_ge(s_done, h * (NC + 1) + NC + 1)
                    head_copies(h + 1)
                    dve.wait_ge(proj_act, by_act(h, V))
                    for _ in conv(2, 0, 8, 4, h * 15 + 23):
                        pass
                dve.wait_ge(rs_done, h * 4 + 4)
                yo = slice(H + h, H + h + 1) if isinstance(h, int) else bass.ds(h + H, 1)
                nc.vector.scalar_tensor_tensor(oT, oT, gw, rs[1], ALU.mult, ALU.mult).then_inc(oy_part, 1)
                dve.wait_ge(oy_part, h + 1)
                nc.vector.tensor_tensor(yT[:, yo].rearrange("p o l -> p (o l)"), oT, zs, ALU.mult).then_inc(oy_done, 1)
                if not last:
                    q_or_k(0, h * 4 + 5)
                    q_or_k(1, h * 4 + 6)

            with dve.Fori(0, H - 1) as h:
                mixer(h, False)
            mixer(H - 1, True)
            if stop == "mixer":
                return
            tail_vector(dve)

        @block.gpsimd
        def _(pool):
            pool.wait_ge(s_const, 32)
            for n in range(2):
                pool.wait_ge(silu_done, n + 1)
                nc.gpsimd.tensor_tensor(sq[n], cv[n], cv[n], ALU.mult).then_inc(sq_done, 1)

            def mixer(h, last):
                for g in range(3):
                    pool.wait_ge(gdn_act, at(ACT_R, h, "grow", g))
                pool.wait_ge(qk_done, h * 2 + 1)
                nc.gpsimd.tensor_tensor(qg, qT, eG, ALU.mult).then_inc(qg_done, 1)
                pool.wait_ge(dexp_done, h + 1)
                nc.gpsimd.tensor_tensor(dTs[0:C], dT[0:C], strict.unsqueeze(1).to_broadcast([C, NC, C]),
                                        ALU.mult).then_inc(dts_done, 1)
                for g in range(3):
                    pool.wait_ge(gdn_dve, at(DVE_R, h, "mtr", g))

                def level(n):
                    nc.gpsimd.tensor_tensor(aL[n % 2][0:C], lM[0:C], lev[:, n, :].unsqueeze(1).to_broadcast([C, NC, C]),
                                            ALU.mult).then_inc(a_done, 1)

                level(0)
                pool.wait_ge(a_done, h * LEVELS + 1)
                pool.wait_ge(dti_done, h + 1)
                pool.wait_ge(dts_done, h + 1)
                nc.gpsimd.tensor_tensor(tI[0:C], ident[0:C, 0:C].unsqueeze(1).to_broadcast([C, NC, C]), aL[0][0:C],
                                        ALU.subtract).then_inc(t0_done, 1)
                for n in range(1, LEVELS):
                    if n == 2:
                        pool.wait_ge(t0_done, h + 1)
                    if n >= 3:
                        pool.wait_ge(gdn_done, at(ROUNDS, h, f"z{n - 2}", 2))
                    if n == 6:
                        pool.wait_ge(proj_dve, by_dve(h, GB))
                        nc.gpsimd.tensor_tensor(sq[0], cv[0], cv[0], ALU.mult).then_inc(sq_done, 1)
                    level(n)
                if not last:
                    pool.wait_ge(sum_done, sums(h, "mix"))
                    pool.wait_ge(silu_done, h * 3 + 4)
                    nc.gpsimd.tensor_tensor(sq[0], cv[0], cv[0], ALU.mult).then_inc(sq_done, 1)
                pool.wait_ge(o_done, h * NC + NC)
                nc.gpsimd.tensor_tensor(sq[1], oT, oT, ALU.mult).then_inc(sq_done, 1)
                if not last:
                    pool.wait_ge(sum_done, sums(h, "o"))
                    pool.wait_ge(silu_done, h * 3 + 5)
                    nc.gpsimd.tensor_tensor(sq[1], cv[1], cv[1], ALU.mult).then_inc(sq_done, 1)

            with pool.Fori(0, H - 1) as h:
                mixer(h, False)
            mixer(H - 1, True)
            if stop == "mixer":
                return
            tail_pool(pool)


def kernel(**inputs):
    import concourse.bacc as bacc
    from concourse.bass_utils import run_bass_kernel_spmd

    a = {k: np.asarray(v) for k, v in inputs.items()}
    w_in = a["w_in"][0]
    cols = [3 * 512 + 3 * 512, 512, 1024, 0, 1536, 2048, 2560]
    order = [(0, Q), (0, K), (0, V)] + [(h + (kind >= Q), kind) for h in range(H) for kind in range(KINDS)]
    wt = np.stack([w_in[:, cols[kind] + 128 * h:cols[kind] + 128 * (h + 1)].reshape(KD, 128, 128).transpose(1, 0, 2)
                   .reshape(128, KD * 128) for h, kind in order[:28]])
    par = np.zeros((128, NPAR), np.float32)

    def put(name, v):
        o, w = PAR[name]
        par[:, o:o + w] = v

    taps = np.zeros((128, 5, 16), np.float32)
    qkv = a["qkv_conv_w"][0].reshape(4, 3, H, 128)
    mix = a["conv_mix_w"][0].reshape(3, H, 128)
    for h in range(H):
        taps[:, h, 0:12] = qkv[:, :, h, :].transpose(2, 1, 0).reshape(128, 12)
        taps[:, h + 1, 12:15] = mix[:, h, :].T
        taps[:, h + 1, 15] = a["conv_mix_norm_w"][0, h * 128:(h + 1) * 128]
    put("taps", taps.reshape(128, 80))
    put("mixw", a["mix_norm_w"][0].reshape(KD, 128).T)
    put("gw", a["gdn_norm_w"][0][:, None])
    put("wab", w_in[:, 3584:3592].reshape(KD, 128, 8).transpose(1, 0, 2).reshape(128, 64))
    wr = np.concatenate([a["w_group"][0], a["w_router"][0].reshape(D, E)], 1)
    put("wr", wr.reshape(KD, 128, 36).transpose(1, 0, 2).reshape(128, KD * 36))
    put("bias", np.concatenate([a["b_group"][0], a["b_router"][0].reshape(E)])[None, :])
    put("alog", a["a_log"][0][None, :])
    put("dt", a["dt_bias"][0][None, :])
    ins = {
        "tokens": np.concatenate([a["meta_tokens"], a["x"][0]], 0),
        "consts": constants(), "par": par, "w_tiles": wt, "w_out": a["w_out"][0],
        "ffn_w": np.broadcast_to(a["ffn_norm_w"][0][None, :], (128, D)),
        "fin_w": np.broadcast_to(a["final_norm_w"][None, :], (128, D)),
        "w_gate": a["w_gate"][0], "w_up": a["w_up"][0], "w_down": a["w_down"][0],
    }
    nc = bacc.Bacc("TRN2", target_bir_lowering=False, num_devices=1)
    arrays, aps = {}, []
    for name, v in ins.items():
        v = np.ascontiguousarray(v)
        arrays["in_" + name] = v
        aps.append(nc.dram_tensor("in_" + name, v.shape, F32, kind="ExternalInput").ap())
    out = nc.dram_tensor("out_y", (L - META, D), F32, kind="ExternalOutput").ap()
    layer_kernel(nc, *aps, out, stop=STOP)
    r = run_bass_kernel_spmd(nc, [arrays], core_ids=[0])
    return r.results[0]["out_y"].reshape(1, L - META, D)
```
